# Optimizing a Trainium2 kernel written in Bass

```python
import jax, jax.numpy as jnp
from jax import lax
import numpy as np

D_MODEL = 1024
BATCH = 1
SEQ = 1024
DEPTH = 1

MLA_HEADS = 8
QK_NOPE = 64
QK_ROPE = 32
V_HEAD = 64
Q_LORA = 384
KV_LORA = 256
ROPE_THETA = 10000.0
Q_BLOCK = 128
LRU_WIDTH = D_MODEL
LRU_BLOCKS = 8
LRU_BLOCK = LRU_WIDTH // LRU_BLOCKS
CONV_WIDTH = 4
LRU_C = 8.0
D_FF = 2816
FFN_RES_WEIGHT = 0.5
NORM_EPS = 1e-6
IN_SPLITS = (Q_LORA, KV_LORA, QK_ROPE, LRU_WIDTH, LRU_WIDTH, D_MODEL, D_MODEL)
D_IN = Q_LORA + KV_LORA + QK_ROPE + 2 * LRU_WIDTH + 2 * D_MODEL

kernel_name = 'hybrid_mla_rglru_macaron_sandwich'

def _rmsnorm(x, g):
    xf = x.astype(jnp.float32)
    y = xf * lax.rsqrt(jnp.mean(xf * xf, axis=-1, keepdims=True) + NORM_EPS)
    return (y * g.astype(jnp.float32)).astype(x.dtype)

def _swiglu(x, w_gate, w_up, w_down):
    return (jax.nn.silu(x @ w_gate) * (x @ w_up)) @ w_down

def _half_ffn(h, pre_g, w_gate, w_up, w_down, post_g):
    y = _swiglu(_rmsnorm(h, pre_g), w_gate, w_up, w_down)
    return h + FFN_RES_WEIGHT * _rmsnorm(y, post_g)

def _rope_tables(positions):
    half = QK_ROPE // 2
    inv_freq = ROPE_THETA ** (-jnp.arange(half, dtype=jnp.float32) / half)
    ang = positions.astype(jnp.float32)[..., None] * inv_freq
    return jnp.cos(ang), jnp.sin(ang)

def _apply_rope(x, cos, sin):
    half = x.shape[-1] // 2
    xf = x.astype(jnp.float32)
    x1, x2 = xf[..., :half], xf[..., half:]
    return jnp.concatenate([x1 * cos - x2 * sin, x2 * cos + x1 * sin], axis=-1).astype(x.dtype)

def _mla_branch(c_q, c_kv, k_rope_raw, positions, q_norm_g, w_uq, kv_norm_g, w_ukv, w_o_mla):
    b, s = c_q.shape[0], c_q.shape[1]
    q = (_rmsnorm(c_q, q_norm_g) @ w_uq).reshape(b, s, MLA_HEADS, QK_NOPE + QK_ROPE)
    kv = (_rmsnorm(c_kv, kv_norm_g) @ w_ukv).reshape(b, s, MLA_HEADS, QK_NOPE + V_HEAD)
    q_nope, q_rope = q[..., :QK_NOPE], q[..., QK_NOPE:]
    k_nope, v = kv[..., :QK_NOPE], kv[..., QK_NOPE:]
    cos, sin = _rope_tables(positions)
    q_rope = _apply_rope(q_rope, cos[:, :, None, :], sin[:, :, None, :])
    k_rope = _apply_rope(k_rope_raw, cos, sin)
    scale = (QK_NOPE + QK_ROPE) ** -0.5
    k_idx = jnp.arange(s)

    def attend(i):
        start = i * Q_BLOCK
        qn = lax.dynamic_slice_in_dim(q_nope, start, Q_BLOCK, axis=1)
        qr = lax.dynamic_slice_in_dim(q_rope, start, Q_BLOCK, axis=1)
        sc = jnp.einsum('bqhd,bkhd->bhqk', qn, k_nope) + jnp.einsum('bqhr,bkr->bhqk', qr, k_rope)
        sc = sc.astype(jnp.float32) * scale
        causal = k_idx[None, :] <= (start + jnp.arange(Q_BLOCK))[:, None]
        sc = jnp.where(causal[None, None], sc, -jnp.inf)
        p = jax.nn.softmax(sc, axis=-1).astype(v.dtype)
        return jnp.einsum('bhqk,bkhd->bqhd', p, v)

    o = lax.map(attend, jnp.arange(s // Q_BLOCK))
    o = jnp.moveaxis(o, 0, 1).reshape(b, s, MLA_HEADS * V_HEAD)
    return o @ w_o_mla

def _lru_combine(left, right):
    a_l, b_l = left
    a_r, b_r = right
    return a_l * a_r, a_r * b_l + b_r

def _rglru_branch(xb, yb, conv_w, conv_b, w_rg, b_rg, w_ig, b_ig, lru_lambda, w_o_lru):
    b, s, w = xb.shape
    xpad = jnp.pad(xb, ((0, 0), (CONV_WIDTH - 1, 0), (0, 0)))
    xc = conv_b + sum(xpad[:, k:k + s] * conv_w[k] for k in range(CONV_WIDTH))
    xg = xc.reshape(b, s, LRU_BLOCKS, LRU_BLOCK)
    r = jax.nn.sigmoid(jnp.einsum('bsgi,gij->bsgj', xg, w_rg) + b_rg).reshape(b, s, w)
    ig = jax.nn.sigmoid(jnp.einsum('bsgi,gij->bsgj', xg, w_ig) + b_ig).reshape(b, s, w)
    log_a = -LRU_C * r.astype(jnp.float32) * jax.nn.softplus(-lru_lambda.astype(jnp.float32))
    a = jnp.exp(log_a)
    gated_x = jnp.sqrt(-jnp.expm1(2.0 * log_a)) * (ig * xc).astype(jnp.float32)
    _, h = lax.associative_scan(_lru_combine, (a, gated_x), axis=1)
    return (h.astype(xb.dtype) * jax.nn.gelu(yb)) @ w_o_lru

def setup_inputs(seed: int = 0) -> dict:
    key = jax.random.key(seed)
    ks = jax.random.split(key, 32)
    L = DEPTH

    def dense(k, fan_in, *shape):
        return jax.random.normal(k, (L,) + shape, jnp.float32) * fan_in ** -0.5

    def gain(k, dim):
        return 1.0 + 0.02 * jax.random.normal(k, (L, dim), jnp.float32)

    def bias(k, *shape):
        return 0.01 * jax.random.normal(k, (L,) + shape, jnp.float32)

    x = jax.random.normal(ks[0], (BATCH, SEQ, D_MODEL), jnp.float32)
    positions = jnp.broadcast_to(jnp.arange(SEQ, dtype=jnp.int32), (BATCH, SEQ))
    a_c = jax.random.uniform(ks[20], (L, LRU_WIDTH), jnp.float32, 0.9, 0.999)
    a0 = a_c ** (1.0 / LRU_C)
    lru_lambda = jnp.log(a0) - jnp.log1p(-a0)
    return {
        'x': x,
        'positions': positions,
        'ffn1_pre_g': gain(ks[1], D_MODEL),
        'ffn1_w_gate': dense(ks[2], D_MODEL, D_MODEL, D_FF),
        'ffn1_w_up': dense(ks[3], D_MODEL, D_MODEL, D_FF),
        'ffn1_w_down': dense(ks[4], D_FF, D_FF, D_MODEL),
        'ffn1_post_g': gain(ks[5], D_MODEL),
        'mix_pre_g': gain(ks[6], D_MODEL),
        'w_in': dense(ks[7], D_MODEL, D_MODEL, D_IN),
        'q_norm_g': gain(ks[8], Q_LORA),
        'w_uq': dense(ks[9], Q_LORA, Q_LORA, MLA_HEADS * (QK_NOPE + QK_ROPE)),
        'kv_norm_g': gain(ks[10], KV_LORA),
        'w_ukv': dense(ks[11], KV_LORA, KV_LORA, MLA_HEADS * (QK_NOPE + V_HEAD)),
        'w_o_mla': dense(ks[12], MLA_HEADS * V_HEAD, MLA_HEADS * V_HEAD, D_MODEL),
        'conv_w': dense(ks[13], CONV_WIDTH, CONV_WIDTH, LRU_WIDTH),
        'conv_b': bias(ks[14], LRU_WIDTH),
        'w_rg': dense(ks[15], LRU_BLOCK, LRU_BLOCKS, LRU_BLOCK, LRU_BLOCK),
        'b_rg': bias(ks[16], LRU_BLOCKS, LRU_BLOCK),
        'w_ig': dense(ks[17], LRU_BLOCK, LRU_BLOCKS, LRU_BLOCK, LRU_BLOCK),
        'b_ig': bias(ks[18], LRU_BLOCKS, LRU_BLOCK),
        'lru_lambda': lru_lambda,
        'w_o_lru': dense(ks[19], LRU_WIDTH, LRU_WIDTH, D_MODEL),
        'w_out': dense(ks[21], D_MODEL, D_MODEL, D_MODEL),
        'mix_post_g': gain(ks[22], D_MODEL),
        'ffn2_pre_g': gain(ks[23], D_MODEL),
        'ffn2_w_gate': dense(ks[24], D_MODEL, D_MODEL, D_FF),
        'ffn2_w_up': dense(ks[25], D_MODEL, D_MODEL, D_FF),
        'ffn2_w_down': dense(ks[26], D_FF, D_FF, D_MODEL),
        'ffn2_post_g': gain(ks[27], D_MODEL),
    }

def reference(x, positions, ffn1_pre_g, ffn1_w_gate, ffn1_w_up, ffn1_w_down, ffn1_post_g,
              mix_pre_g, w_in, q_norm_g, w_uq, kv_norm_g, w_ukv, w_o_mla,
              conv_w, conv_b, w_rg, b_rg, w_ig, b_ig, lru_lambda, w_o_lru, w_out, mix_post_g,
              ffn2_pre_g, ffn2_w_gate, ffn2_w_up, ffn2_w_down, ffn2_post_g):
    split_points = np.cumsum(IN_SPLITS)[:-1].tolist()
    h = x
    for l in range(DEPTH):
        h = _half_ffn(h, ffn1_pre_g[l], ffn1_w_gate[l], ffn1_w_up[l], ffn1_w_down[l], ffn1_post_g[l])
        u = _rmsnorm(h, mix_pre_g[l])
        c_q, c_kv, k_rope_raw, xb, yb, gate_mla, gate_lru = jnp.split(u @ w_in[l], split_points, axis=-1)
        o_mla = _mla_branch(c_q, c_kv, k_rope_raw, positions, q_norm_g[l], w_uq[l],
                            kv_norm_g[l], w_ukv[l], w_o_mla[l])
        o_lru = _rglru_branch(xb, yb, conv_w[l], conv_b[l], w_rg[l], b_rg[l], w_ig[l], b_ig[l],
                              lru_lambda[l], w_o_lru[l])
        merged = jax.nn.sigmoid(gate_mla) * o_mla + jax.nn.sigmoid(gate_lru) * o_lru
        h = h + _rmsnorm(merged @ w_out[l], mix_post_g[l])
        h = _half_ffn(h, ffn2_pre_g[l], ffn2_w_gate[l], ffn2_w_up[l], ffn2_w_down[l], ffn2_post_g[l])
    return h


_drawn_inputs = setup_inputs


def setup_inputs(seed=0):
    import zlib

    import numpy as np

    out = dict(_drawn_inputs(seed))
    spreads = {}
    factors = {'ffn1_pre_g': 3.095,
     'ffn1_post_g': 4.582,
     'q_norm_g': 8.0,
     'kv_norm_g': 8.0,
     'b_rg': 200.0,
     'b_ig': 200.0,
     'mix_post_g': 11.193,
     'ffn2_pre_g': 20.08,
     'ffn2_post_g': 139.809,
     'conv_b': 64.0,
     'w_rg': 31.584,
     'lru_lambda': 25.28,
     'conv_w': 8.0,
     'w_ig': 8.0,
     'w_o_lru': 8.0}
    for name, (base, spread) in spreads.items():
        noise = np.random.default_rng([zlib.crc32(name.encode()), seed]).standard_normal(out[name].shape)
        drawn = base * np.exp(spread * noise) if base else spread * noise
        out[name] = __import__('jax').numpy.asarray(drawn.astype(out[name].dtype))
    for name, factor in factors.items():
        out[name] = (out[name] * factor).astype(out[name].dtype)
    return out
```

```python
from contextlib import ExitStack

import concourse.bass as bass
from concourse import mybir

F32 = mybir.dt.float32
F32R = mybir.dt.float32r
I32 = mybir.dt.int32
ALU = mybir.AluOpType
ACT = mybir.ActivationFunctionType
AX_X = mybir.AxisListType.X

P = 128
SEQ = 1024
D = 1024
DK = D // P
NT = SEQ // P
HALF = 512
D_FF = 2816
PAIRS = D_FF // (2 * P)
HEADS, NOPE, ROPE, VH = 8, 64, 32, 64
QK = NOPE + ROPE
Q_LORA, KV_LORA = 384, 256
QC, KC = Q_LORA // P, KV_LORA // P
LAT = Q_LORA + KV_LORA + ROPE
EPS = 1e-6


class Core:

    def __init__(self, nc, ctx):
        self.nc, self.ctx = nc, ctx
        self.sems, self.round = ExitStack(), []

    def sem(self, name):
        s = self.sems.enter_context(self.nc.semaphore(name))
        self.round.append(s)
        return s

    def recycle(self):
        with self.nc.Block() as block:
            @block.gpsimd
            def _(pool):
                for s in self.round:
                    pool.sem_clear(s)
        self.sems.close()
        self.sems, self.round = ExitStack(), []

    def keep(self, name, shape, dtype=F32):
        return self.ctx.enter_context(self.nc.sbuf_tensor(name, shape, dtype))


def as_f32(ap):
    return ap.bitcast(F32)


def mm3(pe, out, lhs, rhs, start, stop):
    (lh, ll), (rh, rl) = lhs, rhs
    pe.matmul(out, lh, rh, start=start, stop=False)
    pe.matmul(out, lh, rl, start=False, stop=False)
    return pe.matmul(out, ll, rh, start=False, stop=stop)


def split_hi(nc, hi, src):
    return nc.scalar.activation(hi, src, ACT.Copy)


def split_lo(nc, lo, src, hi):
    return nc.vector.tensor_tensor(lo, src, as_f32(hi), ALU.subtract)


def down_tiles(pe, c, tile_wait, d_tile):
    for j in range(2 * NT):
        t, dh = j // 2, j % 2
        tile_wait(j)
        out = c.ps[:, 4 + j % 4, :]
        for i, slot in ((0, 2), (1, 0)):
            lhs = (c.h_hi[:, i, t * P:(t + 1) * P], c.h_lo[:, i, t * P:(t + 1) * P])
            rhs = tuple(w[:, slot, dh * HALF:(dh + 1) * HALF] for w in (c.w_hi, c.w_lo))
            last = mm3(pe, out, lhs, rhs, i == 0, i == 1)
        last.then_inc(d_tile, 1)


def ffn_hidden(c, tag, w_gate, w_up, w_down):
    nc = c.nc
    gate_dram = w_gate.rearrange("(k p) f -> p k f", p=P)
    up_dram = w_up.rearrange("(k p) f -> p k f", p=P)
    down_dram = w_down.rearrange("(f p) d -> p f d", p=P)
    raw_gate, raw_up, raw_down = c.raw_gate, c.raw_up, c.raw_down
    gate_in, up_in, down_in = c.sem(tag + "gate_in"), c.sem(tag + "up_in"), c.sem(tag + "down_in")
    w_hi_done, w_split = c.sem(tag + "w_hi_done"), c.sem(tag + "w_split")
    gate_done, up_done = c.sem(tag + "gate_done"), c.sem(tag + "up_done")
    silu_done, h_done = c.sem(tag + "silu_done"), c.sem(tag + "h_done")
    h_hi_done, h_split = c.sem(tag + "h_hi_done"), c.sem(tag + "h_split")
    d_tile = c.sem(tag + "d_tile")
    y_done = c.sem(tag + "y_done")

    with nc.Block() as block:
        @block.sync
        def _(sp):
            def load(raw, dram, b, signal):
                sp.dma_start(raw[:, :, :], dram[:, :, bass.ts(b, 2 * P)]).then_inc(signal, 16)

            def load_down(b):
                sp.dma_start(raw_down[:, :, :], down_dram[:, bass.ts(b, 2), :]).then_inc(down_in, 16)

            load(raw_gate, gate_dram, 0, gate_in)
            load(raw_up, up_dram, 0, up_in)
            load_down(0)
            with sp.Fori(1, PAIRS) as b:
                sp.wait_ge(w_split, b * 6 - 3)
                load(raw_gate, gate_dram, b, gate_in)
                sp.wait_ge(w_split, b * 6 - 2)
                load(raw_up, up_dram, b, up_in)
                sp.wait_ge(w_split, b * 6 + 2)
                load_down(b)

        def raw_of(kind, i):
            if kind == "down":
                return raw_down[:, i, :]
            return (raw_gate if kind == "gate" else raw_up)[:, :, i * P:(i + 1) * P]

        def slot_of(kind, i):
            return {"gate0": 0, "up0": 1, "down0": 2, "down1": 0, "gate1": 1, "up1": 2}[kind + str(i)]

        def slot(w, kind, i):
            s = w[:, slot_of(kind, i), :]
            return s if kind == "down" else s.rearrange("p (k f) -> p k f", k=DK)

        @block.scalar
        def _(act):
            def hi(kind, i, pair, free):
                act.wait_ge({"gate": gate_in, "up": up_in, "down": down_in}[kind], 16 * (pair + 1))
                if free is not None:
                    act.wait_ge(*free)
                split_hi(nc, slot(c.w_hi, kind, i), raw_of(kind, i)).then_inc(w_hi_done, 1)

            def silu(b, f):
                for half in range(2):
                    u = 4 * b + 2 * f + half
                    act.wait_ge(gate_done, u + 1)
                    if not (isinstance(b, int) and b == 0 and f == 0):
                        act.wait_ge(h_done, u - 1)
                    nc.scalar.activation(c.silu[:, half, :], c.ps[:, 4 * f + half, :], ACT.Silu)\
                        .then_inc(silu_done, 1)

            def h_hi(b, f):
                for half in range(2):
                    act.wait_ge(h_done, 4 * b + 2 * f + half + 1)
                    if not isinstance(b, int) or b > 0:
                        act.wait_ge(d_tile, b * 16)
                    split_hi(nc, c.h_hi[:, f, bass.ts(half, HALF)], c.h32[:, half, :]).then_inc(h_hi_done, 1)

            hi("gate", 0, 0, None)
            hi("up", 0, 0, None)
            silu(0, 0)
            hi("gate", 1, 0, (up_done, 2))
            h_hi(0, 0)
            hi("up", 1, 0, None)
            hi("gate", 0, 1, (gate_done, 2))
            silu(0, 1)
            hi("up", 0, 1, (gate_done, 4))
            h_hi(0, 1)

            def body(b, last):
                hi("down", 0, b - 1, (up_done, b * 4))
                silu(b, 0)
                hi("down", 1, b - 1, (gate_done, b * 4 + 2))
                hi("gate", 1, b, (up_done, b * 4 + 2))
                h_hi(b, 0)
                hi("up", 1, b, (d_tile, b * 16))
                if not last:
                    hi("gate", 0, b + 1, (d_tile, b * 16))
                silu(b, 1)
                if not last:
                    hi("up", 0, b + 1, (gate_done, b * 4 + 4))
                h_hi(b, 1)

            with act.Fori(1, PAIRS - 1) as b:
                body(b, False)
            body(PAIRS - 1, True)
            hi("down", 0, PAIRS - 1, (up_done, 4 * PAIRS))
            hi("down", 1, PAIRS - 1, (gate_done, 4 * PAIRS - 2))

        @block.vector
        def _(dve):
            def lo(kind, i, n):
                dve.wait_ge(w_hi_done, n + 1)
                split_lo(nc, slot(c.w_lo, kind, i), raw_of(kind, i), slot(c.w_hi, kind, i)).then_inc(w_split, 1)

            def hidden(b, f):
                for half in range(2):
                    u = 4 * b + 2 * f + half
                    dve.wait_ge(silu_done, u + 1)
                    dve.wait_ge(up_done, u + 1)
                    if not (isinstance(b, int) and b == 0 and f == 0):
                        dve.wait_ge(h_split, u - 1)
                    nc.vector.tensor_tensor(c.h32[:, half, :], c.silu[:, half, :], c.ps[:, 4 * f + 2 + half, :],
                                            ALU.mult).then_inc(h_done, 1)

            def h_lo(b, f):
                for half in range(2):
                    dve.wait_ge(h_hi_done, 4 * b + 2 * f + half + 1)
                    cols = bass.ts(half, HALF)
                    split_lo(nc, c.h_lo[:, f, cols], c.h32[:, half, :], c.h_hi[:, f, cols]).then_inc(h_split, 1)

            nc.vector.memset(c.y[:, :, :], 0.0).then_inc(y_done, 1)
            lo("gate", 0, 0)
            lo("up", 0, 1)
            hidden(0, 0)
            lo("gate", 1, 2)
            h_lo(0, 0)
            lo("up", 1, 3)
            lo("gate", 0, 4)
            lo("up", 0, 5)
            hidden(0, 1)
            h_lo(0, 1)

            def body(b, last):
                lo("down", 0, b * 6)
                lo("down", 1, b * 6 + 1)
                hidden(b, 0)
                lo("gate", 1, b * 6 + 2)
                dve.wait_ge(y_done, b * 16 - 15)
                for j in range(2 * NT):
                    dve.wait_ge(d_tile, b * 16 + (j - 15))
                    ysl = c.y[:, j // 2, bass.ts(j % 2, HALF)]
                    nc.vector.tensor_tensor(ysl, c.ps[:, 4 + j % 4, :], ysl, ALU.add).then_inc(y_done, 1)
                h_lo(b, 0)
                lo("up", 1, b * 6 + 3)
                if not last:
                    lo("gate", 0, b * 6 + 4)
                    lo("up", 0, b * 6 + 5)
                hidden(b, 1)
                h_lo(b, 1)

            with dve.Fori(1, PAIRS - 1) as b:
                body(b, False)
            body(PAIRS - 1, True)
            lo("down", 0, PAIRS * 6 - 2)
            lo("down", 1, PAIRS * 6 - 1)

        @block.tensor
        def _(pe):
            def project(kind, i, done):
                s = slot_of(kind, i)
                for half in range(2):
                    bank = 4 * i + (2 if kind == "up" else 0) + half
                    for k in range(DK):
                        lhs = tuple(w[:, s, k * P:(k + 1) * P] for w in (c.w_hi, c.w_lo))
                        rhs = tuple(u[:, k, half * HALF:(half + 1) * HALF] for u in (c.u_hi, c.u_lo))
                        last = mm3(pe, c.ps[:, bank, :], lhs, rhs, k == 0, k == DK - 1)
                    last.then_inc(done, 1)

            def gate_up(b, i, n):
                pe.wait_ge(w_split, n + 1)
                if not isinstance(b, int) or b > 0:
                    if i == 0:
                        pe.wait_ge(silu_done, b * 4 - 2)
                    else:
                        pe.wait_ge(y_done, b * 16 - 1)
                project("gate", i, gate_done)
                pe.wait_ge(w_split, n + 2)
                if not isinstance(b, int) or b > 0:
                    if i == 0:
                        pe.wait_ge(h_done, b * 4 - 2)
                    else:
                        pe.wait_ge(y_done, b * 16 + 1)
                project("up", i, up_done)

            gate_up(0, 0, 0)
            gate_up(0, 1, 2)
            with pe.Fori(1, PAIRS) as b:
                gate_up(b, 0, b * 6 - 2)
                pe.wait_ge(w_split, b * 6 + 2)
                pe.wait_ge(h_split, b * 4)

                def tile_wait(j):
                    if j == 0:
                        pe.wait_ge(h_done, b * 4)
                    elif j >= 4:
                        pe.wait_ge(y_done, b * 16 + (j - 18))
                down_tiles(pe, c, tile_wait, d_tile)
                gate_up(b, 1, b * 6 + 2)


def norm_stage(c, tag, x_dram=None, down=False, post_gain=None, pre_gain=None, res_gain=1.0, store=None):
    nc = c.nc
    gain_in = c.sem(tag + "gain_in")
    x_in = [c.sem(f"{tag}x_in{t}") for t in range(NT if x_dram is not None else 0)]
    d_tile, y_done = c.sem(tag + "d_tile"), c.sem(tag + "y_done")
    sq_y, rs_y, scaled_y, gained_y, res_done = (c.sem(tag + n) for n in ("sq_y", "rs_y", "scaled_y", "gained_y", "res_done"))
    sq_r, rs_r, scaled_r, gained_r = (c.sem(tag + n) for n in ("sq_r", "rs_r", "scaled_r", "gained_r"))
    turned, u_hi_done, u_split, stored = (c.sem(tag + n) for n in ("turned", "u_hi_done", "u_split", "stored"))
    power, eps_done, gain_half = c.sem(tag + "power"), c.sem(tag + "eps_done"), c.sem(tag + "gain_half")
    post, pre = post_gain is not None, pre_gain is not None

    with ExitStack() as own:
        def sb(name, shape):
            return own.enter_context(nc.sbuf_tensor(tag + name, shape, F32))
        gains = sb("gains", [P, 2, D])
        squares = sb("squares", [P, 2, D])
        sums = sb("sums", [P, 2, NT])
        means = sb("means", [P, 2, NT])
        rstd = sb("rstd", [P, 2, NT])
        expo = sb("expo", [P, 1])
        block = own.enter_context(nc.Block())

        @block.sync
        def _(sp):
            if x_dram is not None:
                for t in range(NT):
                    sp.dma_start(c.res[:, t, :], x_dram[t * P:(t + 1) * P, :]).then_inc(x_in[t], 16)
                    if t == 0 and pre:
                        sp.dma_start(gains[:, 1, :], pre_gain.partition_broadcast(P)).then_inc(gain_in, 16)
            elif pre:
                sp.dma_start(gains[:, 1, :], pre_gain.partition_broadcast(P)).then_inc(gain_in, 16)
            if post:
                sp.dma_start(gains[:, 0, :], post_gain.partition_broadcast(P)).then_inc(gain_in, 16)
            if store is not None:
                for t in range(NT):
                    sp.wait_ge(res_done, t + 1)
                    sp.dma_start(store[t * P:(t + 1) * P, :], c.res[:, t, :]).then_inc(stored, 16)
                sp.wait_ge(stored, 16 * NT)

        @block.tensor
        def _(pe):
            if down:
                down_tiles(pe, c, lambda j: pe.wait_ge(y_done, j - 3) if j >= 4 else None, d_tile)
            if pre:
                for t in range(NT):
                    pe.wait_ge(gained_r, t + 1)
                    if t >= 2:
                        pe.wait_ge(u_split, t - 1)
                    b = 2 * (t % 2)
                    for k in range(DK):
                        last = pe.transpose(c.ps[:, b + k // 4, (k % 4) * P:(k % 4 + 1) * P],
                                            c.y[:, t, k * P:(k + 1) * P], c.ident[:, :])
                    last.then_inc(turned, 1)

        @block.scalar
        def _(act):
            def square(t, src, which, signal):
                if t > 0:
                    act.wait_ge(signal, t)
                nc.scalar.activation(squares[:, which, :], src, ACT.Square, accum_out=sums[:, which, t:t + 1]).then_inc(signal, 1)

            for s in range(NT + 6):
                if post and s < NT:
                    if down:
                        act.wait_ge(y_done, 2 * s + 2)
                    square(s, c.y[:, s, :], 0, sq_y)
                t = s - 1
                if post and 0 <= t < NT:
                    act.wait_ge(rs_y, t + 1)
                    act.wait_ge(sq_y, t + 1)
                    nc.scalar.activation(c.y[:, t, :], c.y[:, t, :], ACT.Copy, scale=rstd[:, 0, t:t + 1]).then_inc(scaled_y, 1)
                t = s - 3
                if pre and 0 <= t < NT:
                    if post:
                        act.wait_ge(res_done, t + 1)
                    else:
                        act.wait_ge(x_in[t], 16)
                    square(t, c.res[:, t, :], 1, sq_r)
                t = s - 4
                if pre and 0 <= t < NT:
                    act.wait_ge(rs_r, t + 1)
                    nc.scalar.activation(c.y[:, t, :], c.res[:, t, :], ACT.Copy, scale=rstd[:, 1, t:t + 1]).then_inc(scaled_r, 1)
                t = s - 6
                if pre and 0 <= t < NT:
                    act.wait_ge(turned, t + 1)
                    b = 2 * (t % 2)
                    split_hi(nc, c.u_hi[:, :, t * P:(t + 1) * P],
                             c.ps[:, b:b + 2, :].rearrange("p b (k f) -> p (b k) f", k=4)).then_inc(u_hi_done, 1)

        @block.gpsimd
        def _(pool):
            nc.gpsimd.memset(expo[:, :], -0.5).then_inc(power, 1)
            pool.wait_ge(power, 1)
            if post:
                pool.wait_ge(gain_in, 16 * (1 + pre))
                nc.gpsimd.tensor_scalar(gains[:, 0, :], gains[:, 0, :], res_gain, 0.0, ALU.mult, ALU.add).then_inc(gain_half, 1)
                pool.wait_ge(gain_half, 1)

            def rstd_of(t, which, signal, out, n):
                pool.wait_ge(signal, t + 1)
                nc.gpsimd.tensor_scalar(means[:, which, t:t + 1], sums[:, which, t:t + 1], 1.0 / D, EPS, ALU.mult,
                                        ALU.add).then_inc(eps_done, 1)
                pool.wait_ge(eps_done, n)
                nc.gpsimd.tensor_tensor(rstd[:, which, t:t + 1], means[:, which, t:t + 1], expo[:, :], ALU.pow)\
                    .then_inc(out, 1)

            n = 0
            for s in range(NT + 5):
                if post and s < NT:
                    n += 1
                    rstd_of(s, 0, sq_y, rs_y, n)
                t = s - 1
                if post and 0 <= t < NT:
                    pool.wait_ge(scaled_y, t + 1)
                    nc.gpsimd.tensor_tensor(c.y[:, t, :], c.y[:, t, :], gains[:, 0, :], ALU.mult).then_inc(gained_y, 1)
                t = s - 3
                if pre and 0 <= t < NT:
                    n += 1
                    rstd_of(t, 1, sq_r, rs_r, n)
                t = s - 4
                if pre and 0 <= t < NT:
                    pool.wait_ge(scaled_r, t + 1)
                    pool.wait_ge(gain_in, 16 * (1 + post))
                    nc.gpsimd.tensor_tensor(c.y[:, t, :], c.y[:, t, :], gains[:, 1, :], ALU.mult).then_inc(gained_r, 1)

        @block.vector
        def _(dve):
            for s in range(NT + 8):
                if down and s < NT:
                    for j in (2 * s, 2 * s + 1):
                        dve.wait_ge(d_tile, j + 1)
                        ysl = c.y[:, s, (j % 2) * HALF:(j % 2 + 1) * HALF]
                        nc.vector.tensor_tensor(ysl, c.ps[:, 4 + j % 4, :], ysl, ALU.add).then_inc(y_done, 1)
                t = s - 2
                if post and 0 <= t < NT:
                    dve.wait_ge(gained_y, t + 1)
                    if x_dram is not None:
                        dve.wait_ge(x_in[t], 16)
                    nc.vector.tensor_tensor(c.res[:, t, :], c.res[:, t, :], c.y[:, t, :], ALU.add).then_inc(res_done, 1)
                t = s - 6
                if pre and 0 <= t < NT:
                    dve.wait_ge(u_hi_done, t + 1)
                    b = 2 * (t % 2)
                    cols = slice(t * P, (t + 1) * P)
                    split_lo(nc, c.u_lo[:, :, cols], c.ps[:, b:b + 2, :].rearrange("p b (k f) -> p (b k) f", k=4),
                             c.u_hi[:, :, cols]).then_inc(u_split, 1)


def ffn_buffers(c, own, tag):
    def sb(name, shape, dtype=F32):
        return own.enter_context(c.nc.sbuf_tensor(tag + name, shape, dtype))
    c.y = sb("y", [P, NT, D])
    c.h_hi, c.h_lo = sb("h_hi", [P, 2, SEQ], F32R), sb("h_lo", [P, 2, SEQ], F32R)
    c.w_hi, c.w_lo = sb("w_hi", [P, 3, 1024], F32R), sb("w_lo", [P, 3, 1024], F32R)


def ffn_streams(c, own, tag):
    def sb(name, shape, dtype=F32):
        return own.enter_context(c.nc.sbuf_tensor(tag + name, shape, dtype))
    c.raw_gate, c.raw_up = sb("raw_gate", [P, DK, 2 * P]), sb("raw_up", [P, DK, 2 * P])
    c.raw_down = sb("raw_down", [P, 2, D])
    c.silu, c.h32 = sb("silu", [P, 2, HALF]), sb("h32", [P, 2, HALF])


ROW_CONV_W, ROW_CONV_B, ROW_B_RG, ROW_B_IG, ROW_LAMBDA, ROW_QG, ROW_KVG = 0, 32, 40, 48, 56, 64, 67
PARAM_ROWS = 69
LRU_C = 8.0
TWO_PI = 6.283185307179586
PI_IN = 3.1415925
TURN = (6.28125, 0.0019340515136718750, TWO_PI - 6.28125 - 0.0019340515136718750)
MAGIC = 1.5 * 2.0 ** 23
THETA = 10000.0
MASKED = -1e30
CONV = 4


def constants(c, a):
    nc = c.nc
    zeroed, made, rows_in, turned = c.sem("c_zeroed"), c.sem("c_made"), c.sem("c_rows_in"), c.sem("c_turned")
    chain, abs_done, exp_done, rated = c.sem("c_chain"), c.sem("c_abs"), c.sem("c_exp"), c.sem("c_rated")
    with ExitStack() as own:
        def sb(name, shape, dtype=F32):
            return own.enter_context(nc.sbuf_tensor("c_" + name, shape, dtype))
        rows = sb("rows", [P, P])
        z, e, s, s2, poly = (sb(n, [P, DK]) for n in ("z", "e", "s", "s2", "poly"))
        block = own.enter_context(nc.Block())

        @block.sync
        def _(sp):
            for row, n, src in ((ROW_CONV_W, CONV * DK, a["conv_w"][0].rearrange("k (c p) -> (k c) p", p=P)),
                                (ROW_CONV_B, DK, a["conv_b"][0].rearrange("(c p) -> c p", p=P)),
                                (ROW_B_RG, DK, a["b_rg"][0]), (ROW_B_IG, DK, a["b_ig"][0]),
                                (ROW_LAMBDA, DK, a["lru_lambda"][0].rearrange("(c p) -> c p", p=P)),
                                (ROW_QG, QC, a["q_norm_g"][0].rearrange("(c p) -> c p", p=P)),
                                (ROW_KVG, KC, a["kv_norm_g"][0].rearrange("(c p) -> c p", p=P))):
                sp.dma_start(rows[row:row + n, :], src).then_inc(rows_in, 16)

        @block.gpsimd
        def _(pool):
            nc.gpsimd.memset(c.ident[:, :], 0.0).then_inc(zeroed, 1)
            pool.wait_ge(zeroed, 1)
            nc.gpsimd.affine_select(out=c.ident[:, :], in_=c.ident[:, :], compare_op=ALU.not_equal, fill=1.0, base=0,
                                    pattern=[[-1, P]], channel_multiplier=1).then_inc(made, 1)

        @block.tensor
        def _(pe):
            pe.wait_ge(made, 1)
            pe.wait_ge(rows_in, 16 * 7)
            pe.transpose(c.ps[:, 0, 0:PARAM_ROWS], rows[0:PARAM_ROWS, :], c.ident[0:PARAM_ROWS, 0:PARAM_ROWS])\
                .then_inc(turned, 1)

        @block.vector
        def _(dve):
            n = 0

            def link(ins):
                nonlocal n
                n += 1
                ins.then_inc(chain, 1)
                dve.wait_ge(chain, n)

            dve.wait_ge(turned, 1)
            link(nc.vector.tensor_copy(c.params[:, :], c.ps[:, 0, 0:PARAM_ROWS]))
            lam = c.params[:, ROW_LAMBDA:ROW_LAMBDA + DK]
            nc.vector.scalar_tensor_tensor(out=z[:, :], in0=lam, scalar=-1.0, in1=lam, op0=ALU.mult, op1=ALU.max)\
                .then_inc(abs_done, 1)
            dve.wait_ge(exp_done, 1)
            link(nc.vector.tensor_scalar(s2[:, :], e[:, :], 2.0, None, ALU.add))
            link(nc.vector.reciprocal(s2[:, :], s2[:, :]))
            link(nc.vector.tensor_tensor(s[:, :], e[:, :], s2[:, :], ALU.mult))
            link(nc.vector.tensor_tensor(s2[:, :], s[:, :], s[:, :], ALU.mult))
            link(nc.vector.memset(poly[:, :], 1.0 / 19))
            for odd in (17, 15, 13, 11, 9, 7, 5, 3, 1):
                link(nc.vector.tensor_tensor(poly[:, :], poly[:, :], s2[:, :], ALU.mult))
                link(nc.vector.tensor_scalar(poly[:, :], poly[:, :], 1.0 / odd, None, ALU.add))
            link(nc.vector.tensor_tensor(poly[:, :], poly[:, :], s[:, :], ALU.mult))
            link(nc.vector.tensor_scalar(poly[:, :], poly[:, :], 2.0, None, ALU.mult))
            link(nc.vector.tensor_scalar(s[:, :], lam, -1.0, 0.0, ALU.mult, ALU.max))
            link(nc.vector.tensor_tensor(poly[:, :], poly[:, :], s[:, :], ALU.add))
            for i, rate in enumerate((-LRU_C, -2 * LRU_C, LRU_C)):
                nc.vector.tensor_scalar(c.rates[:, i, :], poly[:, :], rate, None, ALU.mult).then_inc(rated, 1)

        @block.scalar
        def _(act):
            act.wait_ge(abs_done, 1)
            nc.scalar.activation(e[:, :], z[:, :], ACT.Exp, scale=-1.0).then_inc(exp_done, 1)


def rope_tables(c, positions):
    nc = c.nc
    zeroed, made, pos_in, turned = c.sem("r_zeroed"), c.sem("r_made"), c.sem("r_pos_in"), c.sem("r_turned")
    chain, ang_done = c.sem("r_chain"), c.sem("r_ang")
    half = ROPE // 2
    with ExitStack() as own:
        def sb(name, shape, dtype=F32):
            return own.enter_context(nc.sbuf_tensor("r_" + name, shape, dtype))
        freq_rows = sb("freq_rows", [1, 2, P])
        one = sb("one", [1, 1])
        mask, ident = sb("mask", [P, P]), c.ident
        freq = sb("freq", [P, 2])
        pos_i = sb("pos_i", [P, SEQ], I32)
        ang, turns = sb("ang", [P, SEQ]), sb("turns", [P, SEQ])
        block = own.enter_context(nc.Block())

        @block.sync
        def _(sp):
            sp.dma_start(pos_i[:, :], positions.partition_broadcast(P)).then_inc(pos_in, 16)

        @block.gpsimd
        def _(pool):
            nc.gpsimd.memset(mask[:, :], 0.0).then_inc(zeroed, 1)
            nc.gpsimd.memset(one[:, :], 1.0).then_inc(zeroed, 1)
            nc.gpsimd.memset(freq_rows[:, :, :], 0.0).then_inc(zeroed, 1)
            pool.wait_ge(zeroed, 3)
            nc.gpsimd.affine_select(out=mask[:, :], in_=mask[:, :], compare_op=ALU.is_ge, fill=MASKED, base=0,
                                    pattern=[[-1, P]], channel_multiplier=1).then_inc(made, 1)
            for i in range(half):
                cols = freq_rows[:, 0, NOPE:P].rearrange("o (g i) -> o g i", i=half)[:, :, i:i + 1]
                nc.gpsimd.memset(cols, float(THETA ** (-i / half))).then_inc(made, 1)
            nc.gpsimd.memset(freq_rows[:, 1, NOPE:QK], TWO_PI / 4).then_inc(made, 1)
            nc.gpsimd.memset(freq_rows[:, 1, QK:QK + half], TWO_PI / 2).then_inc(made, 1)

        @block.tensor
        def _(pe):
            pe.wait_ge(made, 3 + half)
            for i in range(2):
                pe.matmul(c.ps[:, i, 0:1], freq_rows[:, i, :], one[:, :], start=True, stop=True).then_inc(turned, 1)

        @block.vector
        def _(dve):
            n = 0

            def link(ins):
                nonlocal n
                n += 1
                ins.then_inc(chain, 1)
                dve.wait_ge(chain, n)

            dve.wait_ge(turned, 2)
            nc.vector.tensor_copy(c.mask_r[:, :], mask[:, :])
            nc.vector.tensor_copy(c.ident_r[:, :], ident[:, :])
            for i in range(2):
                link(nc.vector.tensor_copy(freq[:, i:i + 1], c.ps[:, i, 0:1]))
            dve.wait_ge(pos_in, 16)
            link(nc.vector.tensor_copy(ang[:, :], pos_i[:, :]))
            link(nc.vector.tensor_scalar(ang[:, :], ang[:, :], freq[:, 0:1], None, ALU.mult))
            link(nc.vector.tensor_scalar(turns[:, :], ang[:, :], 1.0 / TWO_PI, MAGIC, ALU.mult, ALU.add))
            link(nc.vector.tensor_scalar(turns[:, :], turns[:, :], -MAGIC, None, ALU.add))
            for part in TURN:
                link(nc.vector.scalar_tensor_tensor(out=ang[:, :], in0=turns[:, :], scalar=-part, in1=ang[:, :],
                                                    op0=ALU.mult, op1=ALU.add))
            link(nc.vector.tensor_scalar(ang[:, :], ang[:, :], freq[:, 1:2], None, ALU.add))
            link(nc.vector.tensor_scalar(turns[:, :], ang[:, :], TWO_PI / 2, -TWO_PI, ALU.is_gt, ALU.mult))
            link(nc.vector.tensor_tensor(ang[:, :], ang[:, :], turns[:, :], ALU.add))
            nc.vector.tensor_scalar(ang[:, :], ang[:, :], PI_IN, -PI_IN, ALU.min, ALU.max).then_inc(ang_done, 1)

        @block.scalar
        def _(act):
            act.wait_ge(ang_done, 1)
            nc.scalar.activation(c.trig[:, :], ang[:, :], ACT.Sin)


def latents(c, tag, w_in):
    nc = c.nc
    raw_in = [c.sem(f"{tag}raw_in{i}") for i in range(4)]
    w_hi_done, w_split, proj_done, squared, rs_done = (c.sem(tag + n) for n in ("w_hi_done", "w_split", "proj_done", "squared", "rs_done"))
    scaled, kr_zero, kr_done, turned, c_hi_done, c_split = (c.sem(tag + n) for n in ("scaled", "kr_zero", "kr_done", "turned", "c_hi_done", "c_split"))
    power, eps_done, chain, rope_hi = c.sem(tag + "power"), c.sem(tag + "eps_done"), c.sem(tag + "chain"), c.sem(tag + "rope_hi")
    with ExitStack() as own:
        def sb(name, shape, dtype=F32):
            return own.enter_context(nc.sbuf_tensor(tag + name, shape, dtype))
        raw = sb("raw", [P, DK, LAT])
        w_hi, w_lo = sb("w_hi", [P, DK, LAT], F32R), sb("w_lo", [P, DK, LAT], F32R)
        lat = sb("lat", [P, 2, Q_LORA + KV_LORA])
        kr = sb("kr", [P, 2, P])
        kr_t = sb("kr_t", [P, SEQ])
        rot = sb("rot", [P, SEQ])
        squares = sb("squares", [P, 2, Q_LORA])
        sums, means, rstd = sb("sums", [P, 2, NT]), sb("means", [P, 2, NT]), sb("rstd", [P, 2, NT])
        expo = sb("expo", [P, 1])
        block = own.enter_context(nc.Block())
        widths = (Q_LORA, KV_LORA)

        def proj(t):
            b = 2 * (t % 2)
            return c.ps[:, b:b + 2, :].rearrange("p b f -> p (b f)")

        @block.sync
        def _(sp):
            view = w_in.rearrange("(k p) f -> p k f", p=P)
            for i in range(4):
                sp.dma_start(raw[:, 2 * i:2 * i + 2, :], view[:, 2 * i:2 * i + 2, 0:LAT]).then_inc(raw_in[i], 16)

        @block.scalar
        def _(act):
            for i in range(4):
                act.wait_ge(raw_in[i], 16)
                split_hi(nc, w_hi[:, 2 * i:2 * i + 2, :], raw[:, 2 * i:2 * i + 2, :]).then_inc(w_hi_done, 1)
            act.wait_ge(kr_zero, 1)
            for s in range(NT + 2):
                if s < NT:
                    act.wait_ge(proj_done, s + 1)
                    for g, (at, w) in enumerate(((0, Q_LORA), (Q_LORA, KV_LORA))):
                        if s > 0:
                            act.wait_ge(squared, 2 * s - 1 + g)
                        nc.scalar.activation(squares[:, g, 0:w], proj(s)[:, at:at + w], ACT.Square,
                                             accum_out=sums[:, g, s:s + 1]).then_inc(squared, 1)
                    if s >= 2:
                        act.wait_ge(turned, s - 1)
                    act.wait_ge(rs_done, s + 1)
                    for g, (at, w) in enumerate(((0, Q_LORA), (Q_LORA, KV_LORA))):
                        nc.scalar.activation(lat[:, s % 2, at:at + w], proj(s)[:, at:at + w], ACT.Copy,
                                             scale=rstd[:, g, s:s + 1]).then_inc(scaled, 1)
                    at, half = Q_LORA + KV_LORA, ROPE // 2
                    for to, w, back in ((NOPE, ROPE, 0), (QK, half, half), (QK + half, half, 0)):
                        ins = nc.scalar.activation(kr[:, s % 2, to:to + w], proj(s)[:, at + back:at + back + w], ACT.Copy)
                    ins.then_inc(kr_done, 1)
                t = s - 1
                if 0 <= t < NT:
                    act.wait_ge(turned, t + 1)
                    cols = slice(t * P, (t + 1) * P)
                    for i in range(QC):
                        nc.scalar.activation(c.cq_hi[:, i, cols], c.ps[:, 4 + 2 * (t % 2), i * P:(i + 1) * P], ACT.Copy,
                                             scale=c.params[:, ROW_QG + i:ROW_QG + i + 1])
                    for i in range(KC):
                        last = nc.scalar.activation(c.ckv_hi[:, i, cols], c.ps[:, 5 + 2 * (t % 2), i * P:(i + 1) * P],
                                                    ACT.Copy, scale=c.params[:, ROW_KVG + i:ROW_KVG + i + 1])
                    last.then_inc(c_hi_done, 1)
            act.wait_ge(chain, 3)
            split_hi(nc, c.kt_hi[NOPE:QK, :], rot[NOPE:QK, :]).then_inc(rope_hi, 1)

        @block.gpsimd
        def _(pool):
            nc.gpsimd.memset(expo[:, :], -0.5).then_inc(power, 1)
            nc.gpsimd.memset(kr[:, :, :], 0.0).then_inc(kr_zero, 1)
            pool.wait_ge(power, 1)
            for t in range(NT):
                pool.wait_ge(squared, 2 * t + 2)
                for g in range(2):
                    nc.gpsimd.tensor_scalar(means[:, g, t:t + 1], sums[:, g, t:t + 1], 1.0 / widths[g], EPS, ALU.mult,
                                            ALU.add).then_inc(eps_done, 1)
                pool.wait_ge(eps_done, 2 * t + 2)
                for g in range(2):
                    last = nc.gpsimd.tensor_tensor(rstd[:, g, t:t + 1], means[:, g, t:t + 1], expo[:, :], ALU.pow)
                last.then_inc(rs_done, 1)

        @block.vector
        def _(dve):
            for i in range(4):
                dve.wait_ge(w_hi_done, i + 1)
                k = slice(2 * i, 2 * i + 2)
                split_lo(nc, w_lo[:, k, :], raw[:, k, :], w_hi[:, k, :]).then_inc(w_split, 1)
            for t in range(NT):
                dve.wait_ge(c_hi_done, t + 1)
                cols = slice(t * P, (t + 1) * P)
                for i in range(QC):
                    nc.vector.scalar_tensor_tensor(
                        out=c.cq_lo[:, i, cols], in0=c.ps[:, 4 + 2 * (t % 2), i * P:(i + 1) * P],
                        scalar=c.params[:, ROW_QG + i:ROW_QG + i + 1], in1=as_f32(c.cq_hi[:, i, cols]),
                        op0=ALU.mult, op1=ALU.subtract)
                for i in range(KC):
                    nc.vector.scalar_tensor_tensor(
                        out=c.ckv_lo[:, i, cols], in0=c.ps[:, 5 + 2 * (t % 2), i * P:(i + 1) * P],
                        scalar=c.params[:, ROW_KVG + i:ROW_KVG + i + 1], in1=as_f32(c.ckv_hi[:, i, cols]),
                        op0=ALU.mult, op1=ALU.subtract)
                nc.vector.tensor_copy(kr_t[NOPE:P, cols], c.ps[NOPE:P, 4 + 2 * (t % 2), QC * P:(QC + 1) * P])\
                    .then_inc(c_split, 1)
            dve.wait_ge(c_split, NT)
            nc.vector.tensor_tensor(rot[NOPE:QK, :], kr_t[QK:P, :], c.trig[QK:P, :], ALU.mult).then_inc(chain, 1)
            nc.vector.tensor_tensor(kr_t[NOPE:QK, :], kr_t[NOPE:QK, :], c.trig[NOPE:QK, :], ALU.mult).then_inc(chain, 1)
            dve.wait_ge(chain, 2)
            nc.vector.tensor_tensor(rot[NOPE:QK, :], kr_t[NOPE:QK, :], rot[NOPE:QK, :], ALU.add).then_inc(chain, 1)
            dve.wait_ge(rope_hi, 1)
            split_lo(nc, c.kt_lo[NOPE:QK, :], rot[NOPE:QK, :], c.kt_hi[NOPE:QK, :])

        @block.tensor
        def _(pe):
            for s in range(NT + 1):
                if s < NT:
                    if s >= 2:
                        pe.wait_ge(scaled, 2 * s - 2)
                        pe.wait_ge(kr_done, s - 1)
                    b = 2 * (s % 2)
                    for k in range(DK):
                        if s == 0 and k % 2 == 0:
                            pe.wait_ge(w_split, k // 2 + 1)
                        lhs = tuple(u[:, k, s * P:(s + 1) * P] for u in (c.u_hi, c.u_lo))
                        mm3(pe, c.ps[:, b, :], lhs, tuple(w[:, k, 0:HALF] for w in (w_hi, w_lo)), k == 0, k == DK - 1)
                        last = mm3(pe, c.ps[:, b + 1, 0:LAT - HALF], lhs, tuple(w[:, k, HALF:LAT] for w in (w_hi, w_lo)),
                                   k == 0, k == DK - 1)
                    last.then_inc(proj_done, 1)
                t = s - 1
                if 0 <= t < NT:
                    pe.wait_ge(scaled, 2 * t + 2)
                    pe.wait_ge(kr_done, t + 1)
                    if t >= 2:
                        pe.wait_ge(c_split, t - 1)
                    for i in range(QC):
                        pe.transpose(c.ps[:, 4 + 2 * (t % 2), i * P:(i + 1) * P], lat[:, t % 2, i * P:(i + 1) * P], c.ident[:, :])
                    pe.transpose(c.ps[:, 4 + 2 * (t % 2), QC * P:(QC + 1) * P], kr[:, t % 2, :], c.ident[:, :])
                    for i in range(KC):
                        last = pe.transpose(c.ps[:, 5 + 2 * (t % 2), i * P:(i + 1) * P],
                                            lat[:, t % 2, (QC + i) * P:(QC + i + 1) * P], c.ident[:, :])
                    last.then_inc(turned, 1)


def values(c, tag, w_ukv):
    nc = c.nc
    raw_in, w_hi_done, w_split = c.sem(tag + "raw_in"), c.sem(tag + "w_hi_done"), c.sem(tag + "w_split")
    v_done, v_hi_done, v_split = c.sem(tag + "v_done"), c.sem(tag + "v_hi_done"), c.sem(tag + "v_split")
    with ExitStack() as own:
        def sb(name, dtype=F32):
            return own.enter_context(nc.sbuf_tensor(tag + name, [P, KC, HEADS, VH], dtype))
        raw, w_hi, w_lo = sb("raw"), sb("w_hi", F32R), sb("w_lo", F32R)
        block = own.enter_context(nc.Block())

        def flat(w, k):
            return w[:, k, :, :].rearrange("p h e -> p (h e)")

        def out(t):
            return c.ps[:, t, :].rearrange("p (h e) -> p h e", e=VH)

        @block.sync
        def _(sp):
            view = w_ukv.rearrange("(k p) (h e) -> p k h e", p=P, h=HEADS)
            for k in range(KC):
                sp.dma_start(raw[:, k, :, :], view[:, k, :, NOPE:NOPE + VH]).then_inc(raw_in, 16)

        @block.scalar
        def _(act):
            act.wait_ge(raw_in, 16 * KC)
            split_hi(nc, w_hi[:, :, :, :], raw[:, :, :, :]).then_inc(w_hi_done, 1)
            for t in range(NT):
                act.wait_ge(v_done, t + 1)
                split_hi(nc, c.v[:, t, :, 0, :], out(t)).then_inc(v_hi_done, 1)

        @block.vector
        def _(dve):
            dve.wait_ge(w_hi_done, 1)
            split_lo(nc, w_lo[:, :, :, :].rearrange("p k h e -> p (k h e)"),
                     raw[:, :, :, :].rearrange("p k h e -> p (k h e)"),
                     w_hi[:, :, :, :].rearrange("p k h e -> p (k h e)")).then_inc(w_split, 1)
            for t in range(NT):
                dve.wait_ge(v_hi_done, t + 1)
                split_lo(nc, c.v[:, t, :, 1, :], out(t), c.v[:, t, :, 0, :]).then_inc(v_split, 1)

        @block.tensor
        def _(pe):
            pe.wait_ge(w_split, 1)
            for t in range(NT):
                for k in range(KC):
                    lhs = tuple(x[:, k, t * P:(t + 1) * P] for x in (c.ckv_hi, c.ckv_lo))
                    last = mm3(pe, c.ps[:, t, :], lhs, (flat(w_hi, k), flat(w_lo, k)), k == 0, k == KC - 1)
                last.then_inc(v_done, 1)


def attention(c, tag, w_uq, w_ukv):
    nc = c.nc
    scale = float(QK) ** -0.5
    half = ROPE // 2
    NB = NT
    names = ("wq_in", "wkv_in", "w_hi_done", "w_split", "q_done", "k_done", "q_rot", "q_sum", "q_hi", "k_hi", "qk_split",
             "pool_split", "s_done", "max_done", "neg_done", "p_done", "pt_done", "pt_hi", "pt_split", "o_done", "inv_done",
             "o_read", "head_done")
    S = {n: c.sem(tag + n) for n in names}
    with ExitStack() as own:
        def sb(name, shape, dtype=F32):
            return own.enter_context(nc.sbuf_tensor(tag + name, shape, dtype))
        raw_q, raw_kv = sb("raw_q", [P, QC, QK]), sb("raw_kv", [P, KC, P])
        wq_hi, wq_lo = sb("wq_hi", [P, QC, P], F32R), sb("wq_lo", [P, QC, P], F32R)
        wkv_hi, wkv_lo = sb("wkv_hi", [P, KC, P], F32R), sb("wkv_lo", [P, KC, P], F32R)
        qt_hi, qt_lo = sb("qt_hi", [P, SEQ], F32R), sb("qt_lo", [P, SEQ], F32R)
        rot, rot2 = sb("rot", [P, SEQ]), sb("rot2", [P, SEQ])
        probs = sb("probs", [P, 2, SEQ])
        pt_hi, pt_lo = sb("pt_hi", [P, NT, P], F32R), sb("pt_lo", [P, NT, P], F32R)
        mx, neg, rs, inv = (sb(n, [P, NB]) for n in ("mx", "neg", "rs", "inv"))
        block = own.enter_context(nc.Block())

        def two(b):
            return c.ps[:, b:b + 2, :].rearrange("p b f -> p (b f)")

        pieces = ((0, QK, 0), (QK, half, NOPE + half), (QK + half, half, NOPE))

        @block.sync
        def _(sp):
            vq = w_uq.rearrange("(k p) (h e) -> p k h e", p=P, h=HEADS)
            vkv = w_ukv.rearrange("(k p) (h e) -> p k h e", p=P, h=HEADS)
            with sp.Fori(0, HEADS) as h:
                sp.wait_ge(S["head_done"], h + 1)
                sp.dma_start(raw_q[:, :, :], vq[:, :, bass.ds(h, 1), :].rearrange("p k o e -> p k (o e)")).then_inc(S["wq_in"], 16)
                sp.dma_start(raw_kv[:, :, :], vkv[:, :, bass.ds(h, 1), :].rearrange("p k o e -> p k (o e)")).then_inc(S["wkv_in"], 16)

        @block.scalar
        def _(act):
            with act.Fori(0, HEADS) as h:
                act.wait_ge(S["head_done"], h + 1)
                act.wait_ge(S["wq_in"], h * 16 + 16)
                for to, w, at in pieces:
                    split_hi(nc, wq_hi[:, :, to:to + w], raw_q[:, :, at:at + w])
                act.wait_ge(S["wkv_in"], h * 16 + 16)
                split_hi(nc, wkv_hi[:, :, :], raw_kv[:, :, :]).then_inc(S["w_hi_done"], 1)
                act.wait_ge(S["q_done"], h * 2 + 2)
                split_hi(nc, qt_hi[0:NOPE, :], two(0)[0:NOPE, :]).then_inc(S["q_hi"], 1)
                act.wait_ge(S["k_done"], h * 2 + 2)
                split_hi(nc, c.kt_hi[0:NOPE, :], two(2)[0:NOPE, :]).then_inc(S["k_hi"], 1)
                act.wait_ge(S["q_sum"], h + 1)
                split_hi(nc, qt_hi[NOPE:QK, :], rot[NOPE:QK, :]).then_inc(S["q_hi"], 1)
                for s in range(NB + 1):
                    if s < NB:
                        w = (s + 1) * P
                        act.wait_ge(S["neg_done"], h * 8 + (s + 1))
                        if s >= 2:
                            act.wait_ge(S["pt_done"], h * 8 + (s - 1))
                        nc.scalar.activation(probs[:, s % 2, 0:w], two(4 + 2 * (s % 2))[:, 0:w], ACT.Exp, bias=neg[:, s:s + 1],
                                             scale=scale, accum_out=rs[:, s:s + 1]).then_inc(S["p_done"], 1)
                    i = s - 1
                    if i >= 0:
                        act.wait_ge(S["pt_done"], h * 8 + (i + 1))
                        if i >= 1:
                            act.wait_ge(S["o_done"], h * 8 + i)
                        split_hi(nc, pt_hi[:, 0:i + 1, :], two(0)[:, 0:(i + 1) * P].rearrange("p (j q) -> p j q", q=P))\
                            .then_inc(S["pt_hi"], 1)

        @block.gpsimd
        def _(pool):
            with pool.Fori(0, HEADS) as h:
                pool.wait_ge(S["q_rot"], h * 2 + 2)
                nc.gpsimd.tensor_tensor(rot[NOPE:QK, :], rot[NOPE:QK, :], rot2[NOPE:QK, :], ALU.add).then_inc(S["q_sum"], 1)

        @block.vector
        def _(dve):
            nc.vector.memset(mx[:, :], 0.0).then_inc(S["head_done"], 1)
            with dve.Fori(0, HEADS) as h:
                dve.wait_ge(S["w_hi_done"], h + 1)
                for to, w, at in pieces:
                    split_lo(nc, wq_lo[:, :, to:to + w], raw_q[:, :, at:at + w], wq_hi[:, :, to:to + w])
                split_lo(nc, wkv_lo[:, :, :], raw_kv[:, :, :], wkv_hi[:, :, :]).then_inc(S["w_split"], 1)
                dve.wait_ge(S["q_done"], h * 2 + 2)
                nc.vector.tensor_tensor(rot2[NOPE:QK, :], two(0)[QK:P, :], c.trig[QK:P, :], ALU.mult).then_inc(S["q_rot"], 1)
                nc.vector.tensor_tensor(rot[NOPE:QK, :], two(0)[NOPE:QK, :], c.trig[NOPE:QK, :], ALU.mult).then_inc(S["q_rot"], 1)
                dve.wait_ge(S["q_hi"], h * 2 + 1)
                split_lo(nc, qt_lo[0:NOPE, :], two(0)[0:NOPE, :], qt_hi[0:NOPE, :])
                dve.wait_ge(S["k_hi"], h + 1)
                split_lo(nc, c.kt_lo[0:NOPE, :], two(2)[0:NOPE, :], c.kt_hi[0:NOPE, :])
                dve.wait_ge(S["q_hi"], h * 2 + 2)
                split_lo(nc, qt_lo[NOPE:QK, :], rot[NOPE:QK, :], qt_hi[NOPE:QK, :]).then_inc(S["qk_split"], 1)
                for s in range(NB + 2):
                    if s < NB:
                        w = (s + 1) * P
                        dve.wait_ge(S["s_done"], h * 8 + (s + 1))
                        nc.vector.tensor_reduce(mx[:, s:s + 1], two(4 + 2 * (s % 2))[:, 0:w], AX_X, ALU.max).then_inc(S["max_done"], 1)
                        dve.wait_ge(S["max_done"], h * 8 + (s + 1))
                        nc.vector.tensor_scalar(neg[:, s:s + 1], mx[:, s:s + 1], -scale, None, ALU.mult).then_inc(S["neg_done"], 1)
                    i = s - 1
                    if 0 <= i < NB:
                        dve.wait_ge(S["pt_hi"], h * 8 + (i + 1))
                        split_lo(nc, pt_lo[:, 0:i + 1, :], two(0)[:, 0:(i + 1) * P].rearrange("p (j q) -> p j q", q=P),
                                 pt_hi[:, 0:i + 1, :]).then_inc(S["pt_split"], 1)
                    i = s - 2
                    if i >= 0:
                        nc.vector.reciprocal(inv[:, i:i + 1], rs[:, i:i + 1]).then_inc(S["inv_done"], 1)
                        dve.wait_ge(S["o_done"], h * 8 + (i + 1))
                        dve.wait_ge(S["inv_done"], h * 8 + (i + 1))
                        last = nc.vector.tensor_scalar(c.o_nat[:, i, bass.ts(h, VH)], c.ps[:, 2 + i % 2, 0:VH], inv[:, i:i + 1],
                                                       None, ALU.mult)
                        last.then_inc(S["o_read"], 1)
                dve.wait_ge(S["o_read"], h * 8 + 8)
                nc.vector.memset(mx[:, 0:1], 0.0).then_inc(S["head_done"], 1)

        @block.tensor
        def _(pe):
            with pe.Fori(0, HEADS) as h:
                pe.wait_ge(S["head_done"], h + 1)
                pe.wait_ge(S["w_split"], h + 1)
                for n, (weights, x, chunks, signal) in enumerate((
                        ((wq_hi, wq_lo), (c.cq_hi, c.cq_lo), QC, S["q_done"]),
                        ((wkv_hi, wkv_lo), (c.ckv_hi, c.ckv_lo), KC, S["k_done"]))):
                    for hf in range(2):
                        for k in range(chunks):
                            last = mm3(pe, c.ps[:, 2 * n + hf, :], tuple(w[:, k, :] for w in weights),
                                       tuple(y[:, k, hf * HALF:(hf + 1) * HALF] for y in x), k == 0, k == chunks - 1)
                        last.then_inc(signal, 1)
                for s in range(NB + 2):
                    if s < NB:
                        if s == 0:
                            pe.wait_ge(S["qk_split"], h + 1)
                        if s >= 2:
                            pe.wait_ge(S["p_done"], h * 8 + (s - 1))
                        q = tuple(x[0:QK, s * P:(s + 1) * P] for x in (qt_hi, qt_lo))
                        for at in range(0, (s + 1) * P, HALF):
                            w = min(HALF, (s + 1) * P - at)
                            out = c.ps[:, 4 + 2 * (s % 2) + at // HALF, 0:w]
                            mm3(pe, out, q, tuple(x[0:QK, at:at + w] for x in (c.kt_hi, c.kt_lo)), True, True)
                        at = s * P % HALF
                        pe.matmul(c.ps[:, 4 + 2 * (s % 2) + s // 4, at:at + P], c.ident_r[:, :], c.mask_r[:, :], start=False,
                                  stop=True, skip_group_check=True).then_inc(S["s_done"], 1)
                    i = s - 1
                    if 0 <= i < NB:
                        pe.wait_ge(S["p_done"], h * 8 + (i + 1))
                        if i >= 1:
                            pe.wait_ge(S["pt_split"], h * 8 + i)
                        for j in range(i + 1):
                            last = pe.transpose(c.ps[:, j // 4, (j % 4) * P:(j % 4 + 1) * P], probs[:, i % 2, j * P:(j + 1) * P],
                                                c.ident[:, :])
                        last.then_inc(S["pt_done"], 1)
                    i = s - 2
                    if i >= 0:
                        pe.wait_ge(S["pt_split"], h * 8 + (i + 1))
                        if i >= 2:
                            pe.wait_ge(S["o_read"], h * 8 + (i - 1))
                        for j in range(i + 1):
                            v = tuple(c.v[:, j, bass.ds(h, 1), z, :].rearrange("p o e -> p (o e)") for z in range(2))
                            last = mm3(pe, c.ps[:, 2 + i % 2, 0:VH], (pt_hi[:, j, :], pt_lo[:, j, :]), v, j == 0, j == i)
                        last.then_inc(S["o_done"], 1)


def turn_heads(c, tag):
    nc = c.nc
    turned, hi_done, split = c.sem(tag + "turned"), c.sem(tag + "hi_done"), c.sem(tag + "split")
    n_chunks = HEADS * VH // P
    with nc.Block() as block:
        @block.tensor
        def _(pe):
            for t in range(NT):
                for i in range(n_chunks):
                    last = pe.transpose(c.ps[:, t, i * P:(i + 1) * P], c.o_nat[:, t, i * P:(i + 1) * P], c.ident[:, :])
                last.then_inc(turned, 1)

        def bank(t):
            return c.ps[:, t, :].rearrange("p (i q) -> p i q", q=P)

        @block.scalar
        def _(act):
            for t in range(NT):
                act.wait_ge(turned, t + 1)
                split_hi(nc, c.o_hi[:, :, t * P:(t + 1) * P], bank(t)).then_inc(hi_done, 1)

        @block.vector
        def _(dve):
            for t in range(NT):
                dve.wait_ge(hi_done, t + 1)
                cols = slice(t * P, (t + 1) * P)
                split_lo(nc, c.o_lo[:, :, cols], bank(t), c.o_hi[:, :, cols]).then_inc(split, 1)


def gated(c, tag, gate_w, branch_w, x, chunks, store=None, addend=None, merged=None):
    nc = c.nc
    names = ("gate_in", "branch_in", "w_hi_done", "w_split", "gate_done", "branch_done", "sig_done", "prod_done", "stored",
             "add_in", "add_done")
    S = {n: c.sem(tag + n) for n in names}
    with ExitStack() as own:
        def sb(name, shape, dtype=F32):
            return own.enter_context(nc.sbuf_tensor(tag + name, shape, dtype))
        raw_g, raw_b = sb("raw_g", [P, DK, P]), sb("raw_b", [P, chunks, P])
        g_hi, g_lo = sb("g_hi", [P, DK, P], F32R), sb("g_lo", [P, DK, P], F32R)
        b_hi, b_lo = sb("b_hi", [P, chunks, P], F32R), sb("b_lo", [P, chunks, P], F32R)
        sig, prod = sb("sig", [P, 2, HALF]), sb("prod", [P, 2, HALF])
        if addend is not None:
            other = sb("other", [P, 2, HALF])
        block = own.enter_context(nc.Block())
        gate_view = gate_w.rearrange("(k p) f -> p k f", p=P)
        branch_view = branch_w.rearrange("(k p) f -> p k f", p=P)

        def looped(eng, body):
            body(0, False)
            with eng.Fori(1, DK - 1) as d:
                body(d, False)
            body(DK - 1, True)

        def later(d):
            return not isinstance(d, int) or d > 0

        @block.sync
        def _(sp):
            def load(d):
                if later(d):
                    sp.wait_ge(S["w_split"], d * 2)
                sp.dma_start(raw_g[:, :, :], gate_view[:, :, bass.ts(d, P)]).then_inc(S["gate_in"], 16)
                sp.dma_start(raw_b[:, :, :], branch_view[:, :, bass.ts(d, P)]).then_inc(S["branch_in"], 16)
                if addend is not None:
                    if later(d):
                        sp.wait_ge(S["add_done"], d * 2)
                    sp.dma_start(other[:, :, :], addend[bass.ts(d, P), :].rearrange("p (a f) -> p a f", a=2))\
                        .then_inc(S["add_in"], 16)

            def save(d):
                sp.wait_ge(S["prod_done"], d * 2 + 2)
                sp.dma_start(store[bass.ts(d, P), :].rearrange("p (a f) -> p a f", a=2), prod[:, :, :]).then_inc(S["stored"], 16)

            load(0)

            def body(d, last):
                if not last:
                    load(d + 1)
                if store is not None:
                    save(d)
            looped(sp, body)
            if store is not None:
                sp.wait_ge(S["stored"], 16 * DK)

        @block.scalar
        def _(act):
            def hi(d):
                act.wait_ge(S["gate_in"], d * 16 + 16)
                if later(d):
                    act.wait_ge(S["gate_done"], d * 2)
                split_hi(nc, g_hi[:, :, :], raw_g[:, :, :]).then_inc(S["w_hi_done"], 1)
                act.wait_ge(S["branch_in"], d * 16 + 16)
                if later(d):
                    act.wait_ge(S["branch_done"], d * 2)
                split_hi(nc, b_hi[:, :, :], raw_b[:, :, :]).then_inc(S["w_hi_done"], 1)

            hi(0)

            def body(d, last):
                for hf in range(2):
                    act.wait_ge(S["gate_done"], d * 2 + (hf + 1))
                    if later(d):
                        act.wait_ge(S["prod_done"], d * 2 + (hf - 1))
                    nc.scalar.activation(sig[:, hf, :], c.ps[:, hf, :], ACT.Sigmoid).then_inc(S["sig_done"], 1)
                if not last:
                    hi(d + 1)
            looped(act, body)

        @block.vector
        def _(dve):
            def lo(d):
                dve.wait_ge(S["w_hi_done"], d * 2 + 1)
                split_lo(nc, g_lo[:, :, :], raw_g[:, :, :], g_hi[:, :, :]).then_inc(S["w_split"], 1)

            def lo_b(d):
                dve.wait_ge(S["w_hi_done"], d * 2 + 2)
                split_lo(nc, b_lo[:, :, :], raw_b[:, :, :], b_hi[:, :, :]).then_inc(S["w_split"], 1)

            lo(0)
            lo_b(0)

            def body(d, last):
                if not last:
                    lo(d + 1)
                for hf in range(2):
                    dve.wait_ge(S["sig_done"], d * 2 + (hf + 1))
                    dve.wait_ge(S["branch_done"], d * 2 + (hf + 1))
                    if later(d) and store is not None:
                        dve.wait_ge(S["stored"], d * 16)
                    if later(d) and store is None:
                        dve.wait_ge(S["add_done"], d * 2 + (hf - 1))
                    nc.vector.tensor_tensor(prod[:, hf, :], sig[:, hf, :], c.ps[:, 2 + hf, :], ALU.mult)\
                        .then_inc(S["prod_done"], 1)
                if not last:
                    lo_b(d + 1)
            looped(dve, body)

        if addend is not None:
            @block.gpsimd
            def _(pool):
                def body(d, last):
                    pool.wait_ge(S["add_in"], d * 16 + 16)
                    for hf in range(2):
                        pool.wait_ge(S["prod_done"], d * 2 + (hf + 1))
                        dst = merged[:, bass.ds(d, 1), hf * HALF:(hf + 1) * HALF].rearrange("p o f -> p (o f)")
                        nc.gpsimd.tensor_tensor(dst, prod[:, hf, :], other[:, hf, :], ALU.add).then_inc(S["add_done"], 1)
                looped(pool, body)

        @block.tensor
        def _(pe):
            def body(d, last):
                pe.wait_ge(S["w_split"], d * 2 + 1)
                for hf in range(2):
                    if later(d):
                        pe.wait_ge(S["sig_done"], d * 2 + (hf - 1))
                    for k in range(DK):
                        ins = mm3(pe, c.ps[:, hf, :], (g_hi[:, k, :], g_lo[:, k, :]),
                                  tuple(u[:, k, hf * HALF:(hf + 1) * HALF] for u in (c.u_hi, c.u_lo)), k == 0, k == DK - 1)
                    ins.then_inc(S["gate_done"], 1)
                pe.wait_ge(S["w_split"], d * 2 + 2)
                for hf in range(2):
                    if later(d):
                        pe.wait_ge(S["prod_done"], d * 2 + (hf - 1))
                    for k in range(chunks):
                        ins = mm3(pe, c.ps[:, 2 + hf, :], (b_hi[:, k, :], b_lo[:, k, :]),
                                  tuple(y[:, k, hf * HALF:(hf + 1) * HALF] for y in x), k == 0, k == chunks - 1)
                    ins.then_inc(S["branch_done"], 1)
            looped(pe, body)


def recurrence(c, tag, w_xb, w_yb, w_rg, w_ig):
    nc = c.nc
    names = ("x_in", "y_in", "gates_in", "w_hi_done", "w_split", "x_done", "y_done", "r_done", "i_done", "conv", "conv_done",
             "xc_hi", "xc_split", "gelu_done", "sig_r", "sig_i", "a_done", "tanh_done", "m_done", "root_done", "ix_done",
             "bx_done", "scan_done", "out_done", "out_hi", "out_split")
    S = {n: c.sem(tag + n) for n in names}
    with ExitStack() as own:
        def sb(name, shape, dtype=F32):
            return own.enter_context(nc.sbuf_tensor(tag + name, shape, dtype))
        raw = {"x": sb("raw_x", [P, DK, P]), "y": sb("raw_y", [P, DK, P]), "g": sb("raw_g", [P, 2, P])}
        w_hi = {"x": sb("x_hi", [P, DK, P], F32R), "y": sb("y_hi", [P, DK, P], F32R), "g": sb("g_hi", [P, 2, P], F32R)}
        w_lo = {"x": sb("x_lo", [P, DK, P], F32R), "y": sb("y_lo", [P, DK, P], F32R), "g": sb("g_lo", [P, 2, P], F32R)}
        xc, gate_y, r, bx, a, a2, hid = (sb(n, [P, SEQ]) for n in ("xc", "gate_y", "r", "bx", "a", "a2", "hid"))
        xc_hi, xc_lo = sb("xc_hi", [P, SEQ], F32R), sb("xc_lo", [P, SEQ], F32R)
        block = own.enter_context(nc.Block())
        order = ("x", "y", "g")

        def two(b):
            return c.ps[:, b:b + 2, :].rearrange("p b f -> p (b f)")

        def col(row, d):
            return c.params[:, bass.ds(d + row, 1)]

        def later(d):
            return not isinstance(d, int) or d > 0

        def looped(eng, body):
            body(0, False)
            with eng.Fori(1, DK - 1) as d:
                body(d, False)
            body(DK - 1, True)

        @block.sync
        def _(sp):
            vx, vy = (w.rearrange("(k p) f -> p k f", p=P) for w in (w_xb, w_yb))

            def load(d):
                for n, (key, signal) in enumerate((("x", "x_in"), ("y", "y_in"), ("g", "gates_in"))):
                    if later(d):
                        sp.wait_ge(S["w_split"], d * 3 + (n - 2))
                    if key == "g":
                        for i, w in enumerate((w_rg, w_ig)):
                            sp.dma_start(raw["g"][:, i, :], w[bass.ds(d, 1), :, :].rearrange("o i j -> (o i) j"))\
                                .then_inc(S[signal], 16)
                    else:
                        sp.dma_start(raw[key][:, :, :], (vx if key == "x" else vy)[:, :, bass.ts(d, P)]).then_inc(S[signal], 16)
            load(0)

            def body(d, last):
                if not last:
                    load(d + 1)
            looped(sp, body)

        @block.scalar
        def _(act):
            def hi(key, d):
                used = {"x": "x_done", "y": "y_done", "g": "i_done"}[key]
                arrived = {"x": "x_in", "y": "y_in", "g": "gates_in"}[key]
                n = 32 if key == "g" else 16
                act.wait_ge(S[arrived], d * n + n)
                if later(d):
                    act.wait_ge(S[used], d * 2)
                split_hi(nc, w_hi[key][:, :, :], raw[key][:, :, :]).then_inc(S["w_hi_done"], 1)

            for key in order:
                hi(key, 0)

            def body(d, last):
                act.wait_ge(S["conv_done"], d + 1)
                if later(d):
                    act.wait_ge(S["i_done"], d * 2)
                split_hi(nc, xc_hi[:, :], xc[:, :]).then_inc(S["xc_hi"], 1)
                if not last:
                    hi("x", d + 1)
                act.wait_ge(S["y_done"], d * 2 + 2)
                if later(d):
                    act.wait_ge(S["out_split"], d + 0)
                nc.scalar.activation(gate_y[:, :], two(2), ACT.Gelu_apprx_tanh).then_inc(S["gelu_done"], 1)
                if not last:
                    hi("y", d + 1)
                act.wait_ge(S["r_done"], d * 2 + 2)
                nc.scalar.activation(r[:, :], two(4), ACT.Sigmoid, bias=col(ROW_B_RG, d)).then_inc(S["sig_r"], 1)
                act.wait_ge(S["i_done"], d * 2 + 2)
                if later(d):
                    act.wait_ge(S["scan_done"], d + 0)
                nc.scalar.activation(bx[:, :], two(6), ACT.Sigmoid, bias=col(ROW_B_IG, d)).then_inc(S["sig_i"], 1)
                if not last:
                    hi("g", d + 1)
                act.wait_ge(S["sig_r"], d + 1)
                nc.scalar.activation(a[:, :], r[:, :], ACT.Exp, scale=c.rates[:, 0, bass.ds(d, 1)])
                nc.scalar.activation(a2[:, :], r[:, :], ACT.Exp, scale=c.rates[:, 1, bass.ds(d, 1)]).then_inc(S["a_done"], 1)
                act.wait_ge(S["a_done"], d + 1)
                nc.scalar.activation(r[:, :], r[:, :], ACT.Tanh, scale=c.rates[:, 2, bass.ds(d, 1)]).then_inc(S["tanh_done"], 1)
                act.wait_ge(S["m_done"], d + 1)
                nc.scalar.activation(r[:, :], r[:, :], ACT.Sqrt).then_inc(S["root_done"], 1)
                act.wait_ge(S["out_done"], d + 1)
                split_hi(nc, c.lru_hi[:, bass.ds(d, 1), :].rearrange("p o f -> p (o f)"), gate_y[:, :]).then_inc(S["out_hi"], 1)
            looped(act, body)

        @block.vector
        def _(dve):
            def lo(n, key, d):
                dve.wait_ge(S["w_hi_done"], d * 3 + (n + 1))
                split_lo(nc, w_lo[key][:, :, :], raw[key][:, :, :], w_hi[key][:, :, :]).then_inc(S["w_split"], 1)

            for n, key in enumerate(order):
                lo(n, key, 0)

            def body(d, last):
                dve.wait_ge(S["x_done"], d * 2 + 2)
                if later(d):
                    dve.wait_ge(S["ix_done"], d + 0)
                taps = CONV - 1
                nc.vector.tensor_scalar(xc[:, :], two(0), col(ROW_CONV_W + taps * DK, d), col(ROW_CONV_B, d),
                                        ALU.mult, ALU.add).then_inc(S["conv"], 1)
                for k in range(taps):
                    back = taps - k
                    dve.wait_ge(S["conv"], d * taps + (k + 1))
                    nc.vector.scalar_tensor_tensor(
                        out=xc[:, back:SEQ], in0=two(0)[:, 0:SEQ - back], scalar=col(ROW_CONV_W + k * DK, d),
                        in1=xc[:, back:SEQ], op0=ALU.mult, op1=ALU.add).then_inc(S["conv_done" if k == taps - 1 else "conv"], 1)
                dve.wait_ge(S["xc_hi"], d + 1)
                split_lo(nc, xc_lo[:, :], xc[:, :], xc_hi[:, :]).then_inc(S["xc_split"], 1)
                if not last:
                    for n, key in enumerate(order):
                        lo(n, key, d + 1)
                dve.wait_ge(S["tanh_done"], d + 1)
                nc.vector.scalar_tensor_tensor(out=r[:, :], in0=a2[:, :], scalar=1.0, in1=r[:, :], op0=ALU.add,
                                               op1=ALU.mult).then_inc(S["m_done"], 1)
                dve.wait_ge(S["bx_done"], d + 1)
                if later(d):
                    dve.wait_ge(S["out_done"], d + 0)
                nc.vector.tensor_tensor_scan(hid[:, :], a[:, :], bx[:, :], 0.0, ALU.mult, ALU.add).then_inc(S["scan_done"], 1)
                dve.wait_ge(S["out_hi"], d + 1)
                one = (slice(None), bass.ds(d, 1), slice(None))
                split_lo(nc, c.lru_lo[one].rearrange("p o f -> p (o f)"), gate_y[:, :],
                         c.lru_hi[one].rearrange("p o f -> p (o f)")).then_inc(S["out_split"], 1)
            looped(dve, body)

        @block.gpsimd
        def _(pool):
            def body(d, last):
                pool.wait_ge(S["sig_i"], d + 1)
                nc.gpsimd.tensor_tensor(bx[:, :], bx[:, :], xc[:, :], ALU.mult).then_inc(S["ix_done"], 1)
                pool.wait_ge(S["root_done"], d + 1)
                pool.wait_ge(S["ix_done"], d + 1)
                nc.gpsimd.tensor_tensor(bx[:, :], bx[:, :], r[:, :], ALU.mult).then_inc(S["bx_done"], 1)
                pool.wait_ge(S["scan_done"], d + 1)
                pool.wait_ge(S["gelu_done"], d + 1)
                nc.gpsimd.tensor_tensor(gate_y[:, :], hid[:, :], gate_y[:, :], ALU.mult).then_inc(S["out_done"], 1)
            looped(pool, body)

        @block.tensor
        def _(pe):
            def body(d, last):
                for n, (key, signal, free) in enumerate((("x", "x_done", "conv_done"), ("y", "y_done", "gelu_done"))):
                    pe.wait_ge(S["w_split"], d * 3 + (n + 1))
                    if later(d):
                        pe.wait_ge(S[free], d + 0)
                    for hf in range(2):
                        for k in range(DK):
                            ins = mm3(pe, c.ps[:, 2 * n + hf, :], (w_hi[key][:, k, :], w_lo[key][:, k, :]),
                                      tuple(u[:, k, hf * HALF:(hf + 1) * HALF] for u in (c.u_hi, c.u_lo)), k == 0, k == DK - 1)
                        ins.then_inc(S[signal], 1)
                pe.wait_ge(S["w_split"], d * 3 + 3)
                pe.wait_ge(S["xc_split"], d + 1)
                for i, (signal, free) in enumerate((("r_done", "sig_r"), ("i_done", "sig_i"))):
                    if later(d):
                        pe.wait_ge(S[free], d + 0)
                    for hf in range(2):
                        cols = slice(hf * HALF, (hf + 1) * HALF)
                        mm3(pe, c.ps[:, 4 + 2 * i + hf, :], (w_hi["g"][:, i, :], w_lo["g"][:, i, :]),
                            (xc_hi[:, cols], xc_lo[:, cols]), True, True).then_inc(S[signal], 1)
            looped(pe, body)


def out_projection(c, tag, w_out, merged):
    nc = c.nc
    raw_in = [c.sem(f"{tag}raw_in{i}") for i in range(2)]
    names = ("m_hi", "m_split", "w_hi_done", "w_split", "w_used", "y_act", "y_dve")
    S = {n: c.sem(tag + n) for n in names}
    with ExitStack() as own:
        def sb(name, shape, dtype=F32):
            return own.enter_context(nc.sbuf_tensor(tag + name, shape, dtype))
        raw = sb("raw", [P, 2, D])
        w_hi, w_lo = c.w_hi, c.w_lo
        block = own.enter_context(nc.Block())
        steps = [(th, k) for th in range(2) for k in range(DK)]

        def evacuate(eng, th):
            eng.wait_ge(S["w_used"], DK * (th + 1))
            for tt in range(4):
                if eng is nc.scalar:
                    nc.scalar.activation(c.y[:, 4 * th + tt, 0:HALF], c.ps[:, 2 * tt, :], ACT.Copy).then_inc(S["y_act"], 1)
                else:
                    nc.vector.tensor_copy(c.y[:, 4 * th + tt, HALF:D], c.ps[:, 2 * tt + 1, :]).then_inc(S["y_dve"], 1)

        @block.sync
        def _(sp):
            view = w_out.rearrange("(k p) f -> p k f", p=P)
            for n, (_, k) in enumerate(steps):
                if n >= 2:
                    sp.wait_ge(S["w_split"], n - 1)
                sp.dma_start(raw[:, n % 2, :], view[:, k, :]).then_inc(raw_in[n % 2], 16)

        @block.scalar
        def _(act):
            for n, (th, k) in enumerate(steps):
                if th == 0:
                    split_hi(nc, c.u_hi[:, k, :], merged[:, k, :]).then_inc(S["m_hi"], 1)
                act.wait_ge(raw_in[n % 2], 16 * (n // 2 + 1))
                if n >= 2:
                    act.wait_ge(S["w_used"], n - 1)
                split_hi(nc, w_hi[:, n % 2, :], raw[:, n % 2, :]).then_inc(S["w_hi_done"], 1)
                if k == 0 and th == 1:
                    evacuate(act, 0)
            evacuate(act, 1)

        @block.vector
        def _(dve):
            for n, (th, k) in enumerate(steps):
                if th == 0:
                    dve.wait_ge(S["m_hi"], k + 1)
                    split_lo(nc, c.u_lo[:, k, :], merged[:, k, :], c.u_hi[:, k, :]).then_inc(S["m_split"], 1)
                dve.wait_ge(S["w_hi_done"], n + 1)
                split_lo(nc, w_lo[:, n % 2, :], raw[:, n % 2, :], w_hi[:, n % 2, :]).then_inc(S["w_split"], 1)
                if th == 1 and k == 0:
                    evacuate(dve, 0)
            evacuate(dve, 1)

        @block.tensor
        def _(pe):
            for n, (th, k) in enumerate(steps):
                if th == 0:
                    pe.wait_ge(S["m_split"], k + 1)
                pe.wait_ge(S["w_split"], n + 1)
                for tt in range(4):
                    t = 4 * th + tt
                    for dh in range(2):
                        if th == 1 and k == 0:
                            pe.wait_ge(S["y_dve" if dh else "y_act"], tt + 1)
                        ins = mm3(pe, c.ps[:, 2 * tt + dh, :], tuple(u[:, k, t * P:(t + 1) * P] for u in (c.u_hi, c.u_lo)),
                                  tuple(w[:, n % 2, dh * HALF:(dh + 1) * HALF] for w in (w_hi, w_lo)), k == 0, k == DK - 1)
                ins.then_inc(S["w_used"], 1)


def hybrid_layer(nc, a, out):
    h1 = nc.dram_tensor("h1_scratch", [SEQ, D], F32, kind="Internal").ap()
    mixed = nc.dram_tensor("mixed_scratch", [D, SEQ], F32, kind="Internal").ap()
    with ExitStack() as ctx:
        c = Core(nc, ctx)
        c.ident = c.keep("ident", [P, P])
        c.params, c.rates = c.keep("params", [P, PARAM_ROWS]), c.keep("rates", [P, 3, DK])
        c.ps = ctx.enter_context(nc.psum_tensor("ps", [P, 8, HALF], F32))
        c.u_hi, c.u_lo = c.keep("u_hi", [P, DK, SEQ], F32R), c.keep("u_lo", [P, DK, SEQ], F32R)

        constants(c, a)
        with ExitStack() as own:
            c.res = own.enter_context(nc.sbuf_tensor("f1_res", [P, NT, D], F32))
            ffn_buffers(c, own, "f1_")
            norm_stage(c, "in_", x_dram=a["x"][0], pre_gain=a["ffn1_pre_g"][0])
            with ExitStack() as streams:
                ffn_streams(c, streams, "f1_")
                ffn_hidden(c, "f1_", a["ffn1_w_gate"][0], a["ffn1_w_up"][0], a["ffn1_w_down"][0])
            norm_stage(c, "mid1_", down=True, post_gain=a["ffn1_post_g"][0], res_gain=0.5,
                       pre_gain=a["mix_pre_g"][0], store=h1)

        c.recycle()
        w_in = a["w_in"][0]
        at_x = LAT
        at_y, at_ga, at_gb = at_x + D, at_x + 2 * D, at_x + 3 * D
        with ExitStack() as own:
            def sb(name, shape, dtype=F32):
                return own.enter_context(nc.sbuf_tensor(name, shape, dtype))
            with ExitStack() as att:
                def sb2(name, shape, dtype=F32):
                    return att.enter_context(nc.sbuf_tensor(name, shape, dtype))
                c.trig = sb2("trig", [P, SEQ])
                c.mask_r, c.ident_r = sb2("mask_r", [P, P], F32R), sb2("ident_r", [P, P], F32R)
                c.cq_hi, c.cq_lo = sb2("cq_hi", [P, QC, SEQ], F32R), sb2("cq_lo", [P, QC, SEQ], F32R)
                c.ckv_hi, c.ckv_lo = sb2("ckv_hi", [P, KC, SEQ], F32R), sb2("ckv_lo", [P, KC, SEQ], F32R)
                c.kt_hi, c.kt_lo = sb2("kt_hi", [P, SEQ], F32R), sb2("kt_lo", [P, SEQ], F32R)
                rope_tables(c, a["positions"][0])
                latents(c, "lat_", w_in)
                c.v = sb2("v", [P, NT, HEADS, 2, VH], F32R)
                values(c, "val_", a["w_ukv"][0])
                c.o_nat = own.enter_context(nc.sbuf_tensor("o_nat", [P, NT, HEADS * VH], F32, side="right"))
                attention(c, "att_", a["w_uq"][0], a["w_ukv"][0])
            c.o_hi, c.o_lo = (sb(n, [P, HEADS * VH // P, SEQ], F32R) for n in ("o_hi", "o_lo"))
            turn_heads(c, "turn_")
            gated(c, "ga_", w_in[:, at_ga:at_ga + D], a["w_o_mla"][0], (c.o_hi, c.o_lo), HEADS * VH // P, store=mixed)

        c.recycle()
        ffn = ExitStack()
        with ExitStack() as own:
            with ExitStack() as lru:
                c.lru_hi, c.lru_lo = (lru.enter_context(nc.sbuf_tensor(n, [P, DK, SEQ], F32R)) for n in ("lru_hi", "lru_lo"))
                recurrence(c, "lru_", w_in[:, at_x:at_x + D], w_in[:, at_y:at_y + D], a["w_rg"][0], a["w_ig"][0])
                merged = own.enter_context(nc.sbuf_tensor("merged", [P, DK, SEQ], F32, side="right"))
                gated(c, "gb_", w_in[:, at_gb:at_gb + D], a["w_o_lru"][0], (c.lru_hi, c.lru_lo), DK, addend=mixed,
                      merged=merged)
            ffn_buffers(c, ffn, "f2_")
            out_projection(c, "out_", a["w_out"][0], merged)
        c.recycle()
        with ffn:
            own = ffn
            c.res = own.enter_context(nc.sbuf_tensor("f3_res", [P, NT, D], F32))
            norm_stage(c, "mid2_", x_dram=h1, post_gain=a["mix_post_g"][0], pre_gain=a["ffn2_pre_g"][0])
            with ExitStack() as streams:
                ffn_streams(c, streams, "f2s_")
                ffn_hidden(c, "f2_", a["ffn2_w_gate"][0], a["ffn2_w_up"][0], a["ffn2_w_down"][0])
            norm_stage(c, "end_", down=True, post_gain=a["ffn2_post_g"][0], res_gain=0.5, store=out[0])


_OUTS = [((1, SEQ, D), "float32")]


def kernel(**inputs):
    import numpy as _np
    import concourse.bacc as _bacc
    from concourse import mybir as _mybir
    from concourse.bass_utils import run_bass_kernel_spmd as _run

    nc = _bacc.Bacc("TRN2", target_bir_lowering=False, num_devices=1)
    arrays, aps = {}, {}
    for name in inputs:
        a = _np.ascontiguousarray(inputs[name])
        arrays[f"in_{name}_dram"] = a
        aps[name] = nc.dram_tensor(f"in_{name}_dram", a.shape, _mybir.dt.from_np(a.dtype), kind="ExternalInput").ap()
    outs = [nc.dram_tensor(f"out_{i}_dram", shape, _mybir.dt.from_np(_np.dtype(dtype)), kind="ExternalOutput").ap()
            for i, (shape, dtype) in enumerate(_OUTS)]
    hybrid_layer(nc, aps, *outs)
    r = _run(nc, [arrays], core_ids=[0])
    got = tuple(r.results[0][f"out_{i}_dram"] for i in range(len(_OUTS)))
    return got[0]
```

```python
from contextlib import ExitStack

import concourse.bass as bass
from concourse import mybir

F32 = mybir.dt.float32
F32R = mybir.dt.float32r
I32 = mybir.dt.int32
ALU = mybir.AluOpType
ACT = mybir.ActivationFunctionType
AX_X = mybir.AxisListType.X

P = 128
SEQ = 1024
D = 1024
DK = D // P
NT = SEQ // P
HALF = 512
D_FF = 2816
PAIRS = D_FF // (2 * P)
HEADS, NOPE, ROPE, VH = 8, 64, 32, 64
QK = NOPE + ROPE
Q_LORA, KV_LORA = 384, 256
QC, KC = Q_LORA // P, KV_LORA // P
LAT = Q_LORA + KV_LORA + ROPE
EPS = 1e-6


class Core:

    def __init__(self, nc, ctx):
        self.nc, self.ctx = nc, ctx
        self.sems, self.round = ExitStack(), []

    def sem(self, name):
        s = self.sems.enter_context(self.nc.semaphore(name))
        self.round.append(s)
        return s

    def recycle(self):
        with self.nc.Block() as block:
            @block.gpsimd
            def _(pool):
                for s in self.round:
                    pool.sem_clear(s)
        self.sems.close()
        self.sems, self.round = ExitStack(), []

    def keep(self, name, shape, dtype=F32):
        return self.ctx.enter_context(self.nc.sbuf_tensor(name, shape, dtype))


def as_f32(ap):
    return ap.bitcast(F32)


def mm3(pe, out, lhs, rhs, start, stop):
    (lh, ll), (rh, rl) = lhs, rhs
    pe.matmul(out, lh, rh, start=start, stop=False)
    pe.matmul(out, lh, rl, start=False, stop=False)
    return pe.matmul(out, ll, rh, start=False, stop=stop)


def split_hi(nc, hi, src):
    return nc.scalar.activation(hi, src, ACT.Copy)


def split_lo(nc, lo, src, hi):
    return nc.vector.tensor_tensor(lo, src, as_f32(hi), ALU.subtract)


def down_tiles(pe, c, tile_wait, d_tile):
    for j in range(2 * NT):
        t, dh = j // 2, j % 2
        tile_wait(j)
        out = c.ps[:, 4 + j % 4, :]
        for i, slot in ((0, 2), (1, 0)):
            lhs = (c.h_hi[:, i, t * P:(t + 1) * P], c.h_lo[:, i, t * P:(t + 1) * P])
            rhs = tuple(w[:, slot, dh * HALF:(dh + 1) * HALF] for w in (c.w_hi, c.w_lo))
            last = mm3(pe, out, lhs, rhs, i == 0, i == 1)
        last.then_inc(d_tile, 1)


def ffn_hidden(c, tag, w_gate, w_up, w_down):
    nc = c.nc
    gate_dram = w_gate.rearrange("(k p) f -> p k f", p=P)
    up_dram = w_up.rearrange("(k p) f -> p k f", p=P)
    down_dram = w_down.rearrange("(f p) d -> p f d", p=P)
    raw_gate, raw_up, raw_down = c.raw_gate, c.raw_up, c.raw_down
    gate_in, up_in, down_in = c.gate_in, c.up_in, c.sem(tag + "down_in")
    w_hi_done, w_split = c.sem(tag + "w_hi_done"), c.sem(tag + "w_split")
    gate_done, up_done = c.sem(tag + "gate_done"), c.sem(tag + "up_done")
    silu_done, h_done = c.sem(tag + "silu_done"), c.sem(tag + "h_done")
    h_hi_done, h_split = c.sem(tag + "h_hi_done"), c.sem(tag + "h_split")
    d_tile = c.sem(tag + "d_tile")
    y_done = c.sem(tag + "y_done")

    with nc.Block() as block:
        @block.sync
        def _(sp):
            def load(raw, dram, b, signal):
                sp.dma_start(raw[:, :, :], dram[:, :, bass.ts(b, 2 * P)]).then_inc(signal, 16)

            def load_down(b):
                sp.dma_start(raw_down[:, :, :], down_dram[:, bass.ts(b, 2), :]).then_inc(down_in, 16)

            load_down(0)
            with sp.Fori(1, PAIRS) as b:
                sp.wait_ge(w_split, b * 6 - 3)
                load(raw_gate, gate_dram, b, gate_in)
                sp.wait_ge(w_split, b * 6 - 2)
                load(raw_up, up_dram, b, up_in)
                sp.wait_ge(w_split, b * 6 + 2)
                load_down(b)

        def raw_of(kind, i):
            if kind == "down":
                return raw_down[:, i, :]
            return (raw_gate if kind == "gate" else raw_up)[:, :, i * P:(i + 1) * P]

        def slot_of(kind, i):
            return {"gate0": 0, "up0": 1, "down0": 2, "down1": 0, "gate1": 1, "up1": 2}[kind + str(i)]

        def slot(w, kind, i):
            s = w[:, slot_of(kind, i), :]
            return s if kind == "down" else s.rearrange("p (k f) -> p k f", k=DK)

        @block.scalar
        def _(act):
            def hi(kind, i, pair, free):
                act.wait_ge({"gate": gate_in, "up": up_in, "down": down_in}[kind], 16 * (pair + 1))
                if free is not None:
                    act.wait_ge(*free)
                split_hi(nc, slot(c.w_hi, kind, i), raw_of(kind, i)).then_inc(w_hi_done, 1)

            def silu(b, f):
                for half in range(2):
                    u = 4 * b + 2 * f + half
                    act.wait_ge(gate_done, u + 1)
                    if not (isinstance(b, int) and b == 0 and f == 0):
                        act.wait_ge(h_done, u - 1)
                    nc.scalar.activation(c.silu[:, half, :], c.ps[:, 4 * f + half, :], ACT.Silu)\
                        .then_inc(silu_done, 1)

            def h_hi(b, f):
                for half in range(2):
                    act.wait_ge(h_done, 4 * b + 2 * f + half + 1)
                    if not isinstance(b, int) or b > 0:
                        act.wait_ge(d_tile, b * 16)
                    split_hi(nc, c.h_hi[:, f, bass.ts(half, HALF)], c.h32[:, half, :]).then_inc(h_hi_done, 1)

            hi("gate", 0, 0, None)
            hi("up", 0, 0, None)
            silu(0, 0)
            hi("gate", 1, 0, (up_done, 2))
            h_hi(0, 0)
            hi("up", 1, 0, None)
            hi("gate", 0, 1, (gate_done, 2))
            silu(0, 1)
            hi("up", 0, 1, (gate_done, 4))
            h_hi(0, 1)

            def body(b, last):
                hi("down", 0, b - 1, (up_done, b * 4))
                silu(b, 0)
                hi("down", 1, b - 1, (gate_done, b * 4 + 2))
                hi("gate", 1, b, (up_done, b * 4 + 2))
                h_hi(b, 0)
                hi("up", 1, b, (d_tile, b * 16))
                if not last:
                    hi("gate", 0, b + 1, (d_tile, b * 16))
                silu(b, 1)
                if not last:
                    hi("up", 0, b + 1, (gate_done, b * 4 + 4))
                h_hi(b, 1)

            with act.Fori(1, PAIRS - 1) as b:
                body(b, False)
            body(PAIRS - 1, True)
            hi("down", 0, PAIRS - 1, (up_done, 4 * PAIRS))
            hi("down", 1, PAIRS - 1, (gate_done, 4 * PAIRS - 2))

        @block.gpsimd
        def _(pool):
            nc.gpsimd.memset(c.y[:, :, :], 0.0).then_inc(y_done, 1)

        @block.vector
        def _(dve):
            def lo(kind, i, n):
                dve.wait_ge(w_hi_done, n + 1)
                split_lo(nc, slot(c.w_lo, kind, i), raw_of(kind, i), slot(c.w_hi, kind, i)).then_inc(w_split, 1)

            def hidden(b, f):
                for half in range(2):
                    u = 4 * b + 2 * f + half
                    dve.wait_ge(silu_done, u + 1)
                    dve.wait_ge(up_done, u + 1)
                    if not (isinstance(b, int) and b == 0 and f == 0):
                        dve.wait_ge(h_split, u - 1)
                    nc.vector.tensor_tensor(c.h32[:, half, :], c.silu[:, half, :], c.ps[:, 4 * f + 2 + half, :],
                                            ALU.mult).then_inc(h_done, 1)

            def h_lo(b, f):
                for half in range(2):
                    dve.wait_ge(h_hi_done, 4 * b + 2 * f + half + 1)
                    cols = bass.ts(half, HALF)
                    split_lo(nc, c.h_lo[:, f, cols], c.h32[:, half, :], c.h_hi[:, f, cols]).then_inc(h_split, 1)

            lo("gate", 0, 0)
            lo("up", 0, 1)
            hidden(0, 0)
            lo("gate", 1, 2)
            h_lo(0, 0)
            lo("up", 1, 3)
            lo("gate", 0, 4)
            lo("up", 0, 5)
            hidden(0, 1)
            h_lo(0, 1)

            def body(b, last):
                lo("down", 0, b * 6)
                lo("down", 1, b * 6 + 1)
                hidden(b, 0)
                lo("gate", 1, b * 6 + 2)
                dve.wait_ge(y_done, b * 16 - 15)
                for j in range(2 * NT):
                    dve.wait_ge(d_tile, b * 16 + (j - 15))
                    ysl = c.y[:, j // 2, bass.ts(j % 2, HALF)]
                    nc.vector.tensor_tensor(ysl, c.ps[:, 4 + j % 4, :], ysl, ALU.add).then_inc(y_done, 1)
                h_lo(b, 0)
                lo("up", 1, b * 6 + 3)
                if not last:
                    lo("gate", 0, b * 6 + 4)
                    lo("up", 0, b * 6 + 5)
                hidden(b, 1)
                h_lo(b, 1)

            with dve.Fori(1, PAIRS - 1) as b:
                body(b, False)
            body(PAIRS - 1, True)
            lo("down", 0, PAIRS * 6 - 2)
            lo("down", 1, PAIRS * 6 - 1)

        @block.tensor
        def _(pe):
            def project(kind, i, done):
                s = slot_of(kind, i)
                for half in range(2):
                    bank = 4 * i + (2 if kind == "up" else 0) + half
                    for k in range(DK):
                        lhs = tuple(w[:, s, k * P:(k + 1) * P] for w in (c.w_hi, c.w_lo))
                        rhs = tuple(u[:, k, half * HALF:(half + 1) * HALF] for u in (c.u_hi, c.u_lo))
                        last = mm3(pe, c.ps[:, bank, :], lhs, rhs, k == 0, k == DK - 1)
                    last.then_inc(done, 1)

            def gate_up(b, i, n):
                pe.wait_ge(w_split, n + 1)
                if not isinstance(b, int) or b > 0:
                    if i == 0:
                        pe.wait_ge(silu_done, b * 4 - 2)
                    else:
                        pe.wait_ge(y_done, b * 16 - 1)
                project("gate", i, gate_done)
                pe.wait_ge(w_split, n + 2)
                if not isinstance(b, int) or b > 0:
                    if i == 0:
                        pe.wait_ge(h_done, b * 4 - 2)
                    else:
                        pe.wait_ge(y_done, b * 16 + 1)
                project("up", i, up_done)

            gate_up(0, 0, 0)
            gate_up(0, 1, 2)
            with pe.Fori(1, PAIRS) as b:
                gate_up(b, 0, b * 6 - 2)
                pe.wait_ge(w_split, b * 6 + 2)
                pe.wait_ge(h_split, b * 4)

                def tile_wait(j):
                    if j == 0:
                        pe.wait_ge(h_done, b * 4)
                    elif j >= 4:
                        pe.wait_ge(y_done, b * 16 + (j - 18))
                down_tiles(pe, c, tile_wait, d_tile)
                gate_up(b, 1, b * 6 + 2)


def norm_stage(c, tag, x_dram=None, down=False, post_gain=None, pre_gain=None, res_gain=1.0, store=None,
               ahead=None):
    nc = c.nc
    gain_in = c.sem(tag + "gain_in")
    x_in = [c.sem(f"{tag}x_in{t}") for t in range(NT if x_dram is not None else 0)]
    d_tile, y_done = c.sem(tag + "d_tile"), c.sem(tag + "y_done")
    sq_y, rs_y, gained_y, res_done = (c.sem(tag + n) for n in ("sq_y", "rs_y", "gained_y", "res_done"))
    sq_r, rs_r, gained_r = (c.sem(tag + n) for n in ("sq_r", "rs_r", "gained_r"))
    turned, u_hi_done, u_split, stored = (c.sem(tag + n) for n in ("turned", "u_hi_done", "u_split", "stored"))
    power, eps_done, gain_half = c.sem(tag + "power"), c.sem(tag + "eps_done"), c.sem(tag + "gain_half")
    post, pre = post_gain is not None, pre_gain is not None

    with ExitStack() as own:
        def sb(name, shape):
            return own.enter_context(nc.sbuf_tensor(tag + name, shape, F32))
        gains = sb("gains", [P, 2, D])
        squares = sb("squares", [P, 2, D])
        sums = sb("sums", [P, 2, NT])
        means = sb("means", [P, 2, NT])
        rstd = sb("rstd", [P, 2, NT])
        expo = sb("expo", [P, 1])
        block = own.enter_context(nc.Block())

        def gained(src, which, t, signal):
            nc.vector.scalar_tensor_tensor(out=c.y[:, t, :], in0=src, scalar=rstd[:, which, t:t + 1],
                                           in1=gains[:, which, :], op0=ALU.mult, op1=ALU.mult).then_inc(signal, 1)

        def add(eng, t):
            eng.wait_ge(gained_y, t + 1)
            if x_dram is not None:
                eng.wait_ge(x_in[t], 16)
            eng.tensor_tensor(c.res[:, t, :], c.res[:, t, :], c.y[:, t, :], ALU.add).then_inc(res_done, 1)

        @block.sync
        def _(sp):
            if post:
                sp.dma_start(gains[:, 0, :], post_gain.partition_broadcast(P)).then_inc(gain_in, 16)
            if x_dram is not None:
                sp.dma_start(c.res[:, 0, :], x_dram[0:P, :]).then_inc(x_in[0], 16)
            if pre:
                sp.dma_start(gains[:, 1, :], pre_gain.partition_broadcast(P)).then_inc(gain_in, 16)
            if x_dram is not None:
                for t in range(1, NT):
                    sp.dma_start(c.res[:, t, :], x_dram[t * P:(t + 1) * P, :]).then_inc(x_in[t], 16)
            if ahead is not None:
                ahead(sp)
            if store is not None:
                for t in range(NT):
                    sp.wait_ge(res_done, t + 1)
                    sp.dma_start(store[t * P:(t + 1) * P, :], c.res[:, t, :]).then_inc(stored, 16)
                sp.wait_ge(stored, 16 * NT)

        @block.tensor
        def _(pe):
            def turn(t):
                pe.wait_ge(gained_r, t + 1)
                if t >= 2:
                    pe.wait_ge(u_split, t - 1)
                b = 2 * (t % 2)
                for k in range(DK):
                    last = pe.transpose(c.ps[:, b + k // 4, (k % 4) * P:(k % 4 + 1) * P],
                                        c.y[:, t, k * P:(k + 1) * P], c.ident[:, :])
                last.then_inc(turned, 1)

            def between(j):
                if pre and j % 2 == 0 and j >= 10:
                    turn(j // 2 - 5)
                if j >= 4:
                    pe.wait_ge(y_done, j - 3)
            if down:
                down_tiles(pe, c, between, d_tile)
            if pre:
                for t in range(NT - 5 if down else 0, NT):
                    turn(t)

        @block.scalar
        def _(act):
            def square(t, src, which, signal):
                if t > 0:
                    act.wait_ge(signal, t)
                nc.scalar.activation(squares[:, which, :], src, ACT.Square, accum_out=sums[:, which, t:t + 1]).then_inc(signal, 1)

            for s in range(NT + 4):
                if post and s < NT:
                    if down:
                        act.wait_ge(y_done, 2 * s + 2)
                    square(s, c.y[:, s, :], 0, sq_y)
                t = s - 2
                if pre and 0 <= t < NT:
                    if post:
                        act.wait_ge(res_done, t + 1)
                    else:
                        act.wait_ge(x_in[t], 16)
                    square(t, c.res[:, t, :], 1, sq_r)
                t = s - 4
                if pre and 0 <= t < NT:
                    act.wait_ge(turned, t + 1)
                    b = 2 * (t % 2)
                    split_hi(nc, c.u_hi[:, :, t * P:(t + 1) * P],
                             c.ps[:, b:b + 2, :].rearrange("p b (k f) -> p (b k) f", k=4)).then_inc(u_hi_done, 1)

        @block.gpsimd
        def _(pool):
            nc.gpsimd.memset(expo[:, :], -0.5).then_inc(power, 1)
            pool.wait_ge(power, 1)
            if post:
                pool.wait_ge(gain_in, 16 * (1 + pre))
                nc.gpsimd.tensor_scalar(gains[:, 0, :], gains[:, 0, :], res_gain, 0.0, ALU.mult, ALU.add).then_inc(gain_half, 1)
                pool.wait_ge(gain_half, 1)

            def rstd_of(t, which, signal, out, n):
                pool.wait_ge(signal, t + 1)
                nc.gpsimd.tensor_scalar(means[:, which, t:t + 1], sums[:, which, t:t + 1], 1.0 / D, EPS, ALU.mult,
                                        ALU.add).then_inc(eps_done, 1)
                pool.wait_ge(eps_done, n)
                nc.gpsimd.tensor_tensor(rstd[:, which, t:t + 1], means[:, which, t:t + 1], expo[:, :], ALU.pow)\
                    .then_inc(out, 1)

            n = 0
            for s in range(NT + 3):
                if post and s < NT:
                    n += 1
                    rstd_of(s, 0, sq_y, rs_y, n)
                t = s - 1
                if post and pre and 0 <= t < NT:
                    add(pool, t)
                t = s - 2
                if pre and 0 <= t < NT:
                    n += 1
                    rstd_of(t, 1, sq_r, rs_r, n)

        @block.vector
        def _(dve):
            for s in range(NT + 5):
                if down and s < NT:
                    for j in (2 * s, 2 * s + 1):
                        dve.wait_ge(d_tile, j + 1)
                        ysl = c.y[:, s, (j % 2) * HALF:(j % 2 + 1) * HALF]
                        nc.vector.tensor_tensor(ysl, c.ps[:, 4 + j % 4, :], ysl, ALU.add).then_inc(y_done, 1)
                t = s - 1
                if post and 0 <= t < NT:
                    dve.wait_ge(rs_y, t + 1)
                    if t == 0:
                        dve.wait_ge(gain_half, 1)
                    gained(c.y[:, t, :], 0, t, gained_y)
                    if not pre:
                        add(dve, t)
                t = s - 3
                if pre and 0 <= t < NT:
                    dve.wait_ge(rs_r, t + 1)
                    if t == 0:
                        dve.wait_ge(gain_in, 16 * (1 + post))
                    gained(c.res[:, t, :], 1, t, gained_r)
                t = s - 4
                if pre and 0 <= t < NT:
                    dve.wait_ge(u_hi_done, t + 1)
                    b = 2 * (t % 2)
                    cols = slice(t * P, (t + 1) * P)
                    split_lo(nc, c.u_lo[:, :, cols], c.ps[:, b:b + 2, :].rearrange("p b (k f) -> p (b k) f", k=4),
                             c.u_hi[:, :, cols]).then_inc(u_split, 1)


def ffn_buffers(c, own, tag):
    def sb(name, shape, dtype=F32):
        return own.enter_context(c.nc.sbuf_tensor(tag + name, shape, dtype))
    c.y = sb("y", [P, NT, D])
    c.h_hi, c.h_lo = sb("h_hi", [P, 2, SEQ], F32R), sb("h_lo", [P, 2, SEQ], F32R)
    c.w_hi, c.w_lo = sb("w_hi", [P, 3, 1024], F32R), sb("w_lo", [P, 3, 1024], F32R)
    c.raw_gate, c.raw_up = sb("raw_gate", [P, DK, 2 * P]), sb("raw_up", [P, DK, 2 * P])


def ffn_ahead(c, tag, w_gate, w_up):
    c.gate_in, c.up_in = c.sem(tag + "gate_in"), c.sem(tag + "up_in")

    def issue(sp):
        for raw, w, signal in ((c.raw_gate, w_gate, c.gate_in), (c.raw_up, w_up, c.up_in)):
            sp.dma_start(raw[:, :, :], w.rearrange("(k p) f -> p k f", p=P)[:, :, 0:2 * P]).then_inc(signal, 16)
    return issue


def ffn_streams(c, own, tag):
    def sb(name, shape, dtype=F32):
        return own.enter_context(c.nc.sbuf_tensor(tag + name, shape, dtype))
    c.raw_down = sb("raw_down", [P, 2, D])
    c.silu, c.h32 = sb("silu", [P, 2, HALF]), sb("h32", [P, 2, HALF])


ROW_CONV_W, ROW_CONV_B, ROW_B_RG, ROW_B_IG, ROW_LAMBDA, ROW_QG, ROW_KVG = 0, 32, 40, 48, 56, 64, 67
PARAM_ROWS = 69
LRU_C = 8.0
TWO_PI = 6.283185307179586
PI_IN = 3.1415925
TURN = (6.28125, 0.0019340515136718750, TWO_PI - 6.28125 - 0.0019340515136718750)
MAGIC = 1.5 * 2.0 ** 23
THETA = 10000.0
MASKED = -1e30
CONV = 4


def constants(c, a):
    nc = c.nc
    zeroed, made, rows_in, turned = c.sem("c_zeroed"), c.sem("c_made"), c.sem("c_rows_in"), c.sem("c_turned")
    chain, abs_done, exp_done, rated = c.sem("c_chain"), c.sem("c_abs"), c.sem("c_exp"), c.sem("c_rated")
    with ExitStack() as own:
        def sb(name, shape, dtype=F32):
            return own.enter_context(nc.sbuf_tensor("c_" + name, shape, dtype))
        rows = sb("rows", [P, P])
        z, e, s, s2, poly = (sb(n, [P, DK]) for n in ("z", "e", "s", "s2", "poly"))
        block = own.enter_context(nc.Block())

        @block.sync
        def _(sp):
            for row, n, src in ((ROW_CONV_W, CONV * DK, a["conv_w"][0].rearrange("k (c p) -> (k c) p", p=P)),
                                (ROW_CONV_B, DK, a["conv_b"][0].rearrange("(c p) -> c p", p=P)),
                                (ROW_B_RG, DK, a["b_rg"][0]), (ROW_B_IG, DK, a["b_ig"][0]),
                                (ROW_LAMBDA, DK, a["lru_lambda"][0].rearrange("(c p) -> c p", p=P)),
                                (ROW_QG, QC, a["q_norm_g"][0].rearrange("(c p) -> c p", p=P)),
                                (ROW_KVG, KC, a["kv_norm_g"][0].rearrange("(c p) -> c p", p=P))):
                sp.dma_start(rows[row:row + n, :], src).then_inc(rows_in, 16)

        @block.gpsimd
        def _(pool):
            nc.gpsimd.memset(c.ident[:, :], 0.0).then_inc(zeroed, 1)
            pool.wait_ge(zeroed, 1)
            nc.gpsimd.affine_select(out=c.ident[:, :], in_=c.ident[:, :], compare_op=ALU.not_equal, fill=1.0, base=0,
                                    pattern=[[-1, P]], channel_multiplier=1).then_inc(made, 1)

        @block.tensor
        def _(pe):
            pe.wait_ge(made, 1)
            pe.wait_ge(rows_in, 16 * 7)
            pe.transpose(c.ps[:, 0, 0:PARAM_ROWS], rows[0:PARAM_ROWS, :], c.ident[0:PARAM_ROWS, 0:PARAM_ROWS])\
                .then_inc(turned, 1)

        @block.vector
        def _(dve):
            n = 0

            def link(ins):
                nonlocal n
                n += 1
                ins.then_inc(chain, 1)
                dve.wait_ge(chain, n)

            dve.wait_ge(turned, 1)
            link(nc.vector.tensor_copy(c.params[:, :], c.ps[:, 0, 0:PARAM_ROWS]))
            lam = c.params[:, ROW_LAMBDA:ROW_LAMBDA + DK]
            nc.vector.scalar_tensor_tensor(out=z[:, :], in0=lam, scalar=-1.0, in1=lam, op0=ALU.mult, op1=ALU.max)\
                .then_inc(abs_done, 1)
            dve.wait_ge(exp_done, 1)
            link(nc.vector.tensor_scalar(s2[:, :], e[:, :], 2.0, None, ALU.add))
            link(nc.vector.reciprocal(s2[:, :], s2[:, :]))
            link(nc.vector.tensor_tensor(s[:, :], e[:, :], s2[:, :], ALU.mult))
            link(nc.vector.tensor_tensor(s2[:, :], s[:, :], s[:, :], ALU.mult))
            link(nc.vector.memset(poly[:, :], 1.0 / 19))
            for odd in (17, 15, 13, 11, 9, 7, 5, 3, 1):
                link(nc.vector.tensor_tensor(poly[:, :], poly[:, :], s2[:, :], ALU.mult))
                link(nc.vector.tensor_scalar(poly[:, :], poly[:, :], 1.0 / odd, None, ALU.add))
            link(nc.vector.tensor_tensor(poly[:, :], poly[:, :], s[:, :], ALU.mult))
            link(nc.vector.tensor_scalar(poly[:, :], poly[:, :], 2.0, None, ALU.mult))
            link(nc.vector.tensor_scalar(s[:, :], lam, -1.0, 0.0, ALU.mult, ALU.max))
            link(nc.vector.tensor_tensor(poly[:, :], poly[:, :], s[:, :], ALU.add))
            for i, rate in enumerate((-LRU_C, -2 * LRU_C, LRU_C)):
                nc.vector.tensor_scalar(c.rates[:, i, :], poly[:, :], rate, None, ALU.mult).then_inc(rated, 1)

        @block.scalar
        def _(act):
            act.wait_ge(abs_done, 1)
            nc.scalar.activation(e[:, :], z[:, :], ACT.Exp, scale=-1.0).then_inc(exp_done, 1)


def rope_tables(c, positions):
    nc = c.nc
    zeroed, made, pos_in, turned = c.sem("r_zeroed"), c.sem("r_made"), c.sem("r_pos_in"), c.sem("r_turned")
    chain, ang_done = c.sem("r_chain"), c.sem("r_ang")
    half = ROPE // 2
    with ExitStack() as own:
        def sb(name, shape, dtype=F32):
            return own.enter_context(nc.sbuf_tensor("r_" + name, shape, dtype))
        freq_rows = sb("freq_rows", [1, 2, P])
        one = sb("one", [1, 1])
        mask, ident = sb("mask", [P, P]), c.ident
        freq = sb("freq", [P, 2])
        pos_i = sb("pos_i", [P, SEQ], I32)
        ang, turns = sb("ang", [P, SEQ]), sb("turns", [P, SEQ])
        block = own.enter_context(nc.Block())

        @block.sync
        def _(sp):
            sp.dma_start(pos_i[:, :], positions.partition_broadcast(P)).then_inc(pos_in, 16)

        @block.gpsimd
        def _(pool):
            nc.gpsimd.memset(mask[:, :], 0.0).then_inc(zeroed, 1)
            nc.gpsimd.memset(one[:, :], 1.0).then_inc(zeroed, 1)
            nc.gpsimd.memset(freq_rows[:, :, :], 0.0).then_inc(zeroed, 1)
            pool.wait_ge(zeroed, 3)
            nc.gpsimd.affine_select(out=mask[:, :], in_=mask[:, :], compare_op=ALU.is_ge, fill=MASKED, base=0,
                                    pattern=[[-1, P]], channel_multiplier=1).then_inc(made, 1)
            for i in range(half):
                cols = freq_rows[:, 0, NOPE:P].rearrange("o (g i) -> o g i", i=half)[:, :, i:i + 1]
                nc.gpsimd.memset(cols, float(THETA ** (-i / half))).then_inc(made, 1)
            nc.gpsimd.memset(freq_rows[:, 1, NOPE:QK], TWO_PI / 4).then_inc(made, 1)
            nc.gpsimd.memset(freq_rows[:, 1, QK:QK + half], TWO_PI / 2).then_inc(made, 1)

        @block.tensor
        def _(pe):
            pe.wait_ge(made, 3 + half)
            for i in range(2):
                pe.matmul(c.ps[:, i, 0:1], freq_rows[:, i, :], one[:, :], start=True, stop=True).then_inc(turned, 1)

        @block.vector
        def _(dve):
            n = 0

            def link(ins):
                nonlocal n
                n += 1
                ins.then_inc(chain, 1)
                dve.wait_ge(chain, n)

            dve.wait_ge(turned, 2)
            nc.vector.tensor_copy(c.mask_r[:, :], mask[:, :])
            nc.vector.tensor_copy(c.ident_r[:, :], ident[:, :])
            for i in range(2):
                link(nc.vector.tensor_copy(freq[:, i:i + 1], c.ps[:, i, 0:1]))
            dve.wait_ge(pos_in, 16)
            link(nc.vector.tensor_copy(ang[:, :], pos_i[:, :]))
            link(nc.vector.tensor_scalar(ang[:, :], ang[:, :], freq[:, 0:1], None, ALU.mult))
            link(nc.vector.tensor_scalar(turns[:, :], ang[:, :], 1.0 / TWO_PI, MAGIC, ALU.mult, ALU.add))
            link(nc.vector.tensor_scalar(turns[:, :], turns[:, :], -MAGIC, None, ALU.add))
            for part in TURN:
                link(nc.vector.scalar_tensor_tensor(out=ang[:, :], in0=turns[:, :], scalar=-part, in1=ang[:, :],
                                                    op0=ALU.mult, op1=ALU.add))
            link(nc.vector.tensor_scalar(ang[:, :], ang[:, :], freq[:, 1:2], None, ALU.add))
            link(nc.vector.tensor_scalar(turns[:, :], ang[:, :], TWO_PI / 2, -TWO_PI, ALU.is_gt, ALU.mult))
            link(nc.vector.tensor_tensor(ang[:, :], ang[:, :], turns[:, :], ALU.add))
            nc.vector.tensor_scalar(ang[:, :], ang[:, :], PI_IN, -PI_IN, ALU.min, ALU.max).then_inc(ang_done, 1)

        @block.scalar
        def _(act):
            act.wait_ge(ang_done, 1)
            nc.scalar.activation(c.trig[:, :], ang[:, :], ACT.Sin)


def latents(c, tag, w_in, w_ukv):
    nc = c.nc
    raw_in = [c.sem(f"{tag}raw_in{i}") for i in range(4)]
    w_hi_done, w_split, proj_done, squared, rs_done = (c.sem(tag + n) for n in ("w_hi_done", "w_split", "proj_done", "squared", "rs_done"))
    scaled, kr_zero, kr_done, turned, c_hi_done, c_split = (c.sem(tag + n) for n in ("scaled", "kr_zero", "kr_done", "turned", "c_hi_done", "c_split"))
    power, eps_done, chain, rope_hi = c.sem(tag + "power"), c.sem(tag + "eps_done"), c.sem(tag + "chain"), c.sem(tag + "rope_hi")
    with ExitStack() as own:
        def sb(name, shape, dtype=F32):
            return own.enter_context(nc.sbuf_tensor(tag + name, shape, dtype))
        raw = sb("raw", [P, DK, LAT])
        w_hi, w_lo = sb("w_hi", [P, DK, LAT], F32R), sb("w_lo", [P, DK, LAT], F32R)
        lat = sb("lat", [P, 2, Q_LORA + KV_LORA])
        kr = sb("kr", [P, 2, P])
        kr_t = sb("kr_t", [P, SEQ])
        rot = sb("rot", [P, SEQ])
        squares = sb("squares", [P, 2, Q_LORA])
        sums, means, rstd = sb("sums", [P, 2, NT]), sb("means", [P, 2, NT]), sb("rstd", [P, 2, NT])
        expo = sb("expo", [P, 1])
        block = own.enter_context(nc.Block())
        widths = (Q_LORA, KV_LORA)

        def proj(t):
            b = 2 * (t % 2)
            return c.ps[:, b:b + 2, :].rearrange("p b f -> p (b f)")

        @block.sync
        def _(sp):
            view = w_in.rearrange("(k p) f -> p k f", p=P)
            for i in range(4):
                sp.dma_start(raw[:, 2 * i:2 * i + 2, :], view[:, 2 * i:2 * i + 2, 0:LAT]).then_inc(raw_in[i], 16)
            view = w_ukv.rearrange("(k p) (h e) -> p k h e", p=P, h=HEADS)
            for k in range(KC):
                sp.dma_start(c.raw_v[:, k, :, :], view[:, k, :, NOPE:NOPE + VH]).then_inc(c.raw_v_in, 16)

        @block.scalar
        def _(act):
            for i in range(4):
                act.wait_ge(raw_in[i], 16)
                split_hi(nc, w_hi[:, 2 * i:2 * i + 2, :], raw[:, 2 * i:2 * i + 2, :]).then_inc(w_hi_done, 1)
            act.wait_ge(kr_zero, 1)
            for s in range(NT + 2):
                if s < NT:
                    act.wait_ge(proj_done, s + 1)
                    for g, (at, w) in enumerate(((0, Q_LORA), (Q_LORA, KV_LORA))):
                        if s > 0:
                            act.wait_ge(squared, 2 * s - 1 + g)
                        nc.scalar.activation(squares[:, g, 0:w], proj(s)[:, at:at + w], ACT.Square,
                                             accum_out=sums[:, g, s:s + 1]).then_inc(squared, 1)
                    if s >= 2:
                        act.wait_ge(turned, s - 1)
                    act.wait_ge(rs_done, s + 1)
                    for g, (at, w) in enumerate(((0, Q_LORA), (Q_LORA, KV_LORA))):
                        nc.scalar.activation(lat[:, s % 2, at:at + w], proj(s)[:, at:at + w], ACT.Copy,
                                             scale=rstd[:, g, s:s + 1]).then_inc(scaled, 1)
                    at, half = Q_LORA + KV_LORA, ROPE // 2
                    for to, w, back in ((NOPE, ROPE, 0), (QK, half, half), (QK + half, half, 0)):
                        ins = nc.scalar.activation(kr[:, s % 2, to:to + w], proj(s)[:, at + back:at + back + w], ACT.Copy)
                    ins.then_inc(kr_done, 1)
                t = s - 1
                if 0 <= t < NT:
                    act.wait_ge(turned, t + 1)
                    cols = slice(t * P, (t + 1) * P)
                    for i in range(QC):
                        nc.scalar.activation(c.cq_hi[:, i, cols], c.ps[:, 4 + 2 * (t % 2), i * P:(i + 1) * P], ACT.Copy,
                                             scale=c.params[:, ROW_QG + i:ROW_QG + i + 1])
                    for i in range(KC):
                        last = nc.scalar.activation(c.ckv_hi[:, i, cols], c.ps[:, 5 + 2 * (t % 2), i * P:(i + 1) * P],
                                                    ACT.Copy, scale=c.params[:, ROW_KVG + i:ROW_KVG + i + 1])
                    last.then_inc(c_hi_done, 1)
            act.wait_ge(chain, 3)
            split_hi(nc, c.kt_hi[NOPE:QK, :], rot[NOPE:QK, :]).then_inc(rope_hi, 1)

        @block.gpsimd
        def _(pool):
            nc.gpsimd.memset(expo[:, :], -0.5).then_inc(power, 1)
            nc.gpsimd.memset(kr[:, :, :], 0.0).then_inc(kr_zero, 1)
            pool.wait_ge(power, 1)
            for t in range(NT):
                pool.wait_ge(squared, 2 * t + 2)
                for g in range(2):
                    nc.gpsimd.tensor_scalar(means[:, g, t:t + 1], sums[:, g, t:t + 1], 1.0 / widths[g], EPS, ALU.mult,
                                            ALU.add).then_inc(eps_done, 1)
                pool.wait_ge(eps_done, 2 * t + 2)
                for g in range(2):
                    last = nc.gpsimd.tensor_tensor(rstd[:, g, t:t + 1], means[:, g, t:t + 1], expo[:, :], ALU.pow)
                last.then_inc(rs_done, 1)

        @block.vector
        def _(dve):
            for i in range(4):
                dve.wait_ge(w_hi_done, i + 1)
                k = slice(2 * i, 2 * i + 2)
                split_lo(nc, w_lo[:, k, :], raw[:, k, :], w_hi[:, k, :]).then_inc(w_split, 1)
            for t in range(NT):
                dve.wait_ge(c_hi_done, t + 1)
                cols = slice(t * P, (t + 1) * P)
                for i in range(QC):
                    nc.vector.scalar_tensor_tensor(
                        out=c.cq_lo[:, i, cols], in0=c.ps[:, 4 + 2 * (t % 2), i * P:(i + 1) * P],
                        scalar=c.params[:, ROW_QG + i:ROW_QG + i + 1], in1=as_f32(c.cq_hi[:, i, cols]),
                        op0=ALU.mult, op1=ALU.subtract)
                for i in range(KC):
                    nc.vector.scalar_tensor_tensor(
                        out=c.ckv_lo[:, i, cols], in0=c.ps[:, 5 + 2 * (t % 2), i * P:(i + 1) * P],
                        scalar=c.params[:, ROW_KVG + i:ROW_KVG + i + 1], in1=as_f32(c.ckv_hi[:, i, cols]),
                        op0=ALU.mult, op1=ALU.subtract)
                nc.vector.tensor_copy(kr_t[NOPE:P, cols], c.ps[NOPE:P, 4 + 2 * (t % 2), QC * P:(QC + 1) * P])\
                    .then_inc(c_split, 1)
            dve.wait_ge(c_split, NT)
            nc.vector.tensor_tensor(rot[NOPE:QK, :], kr_t[QK:P, :], c.trig[QK:P, :], ALU.mult).then_inc(chain, 1)
            nc.vector.tensor_tensor(kr_t[NOPE:QK, :], kr_t[NOPE:QK, :], c.trig[NOPE:QK, :], ALU.mult).then_inc(chain, 1)
            dve.wait_ge(chain, 2)
            nc.vector.tensor_tensor(rot[NOPE:QK, :], kr_t[NOPE:QK, :], rot[NOPE:QK, :], ALU.add).then_inc(chain, 1)
            dve.wait_ge(rope_hi, 1)
            split_lo(nc, c.kt_lo[NOPE:QK, :], rot[NOPE:QK, :], c.kt_hi[NOPE:QK, :])

        @block.tensor
        def _(pe):
            for s in range(NT + 1):
                if s < NT:
                    if s >= 2:
                        pe.wait_ge(scaled, 2 * s - 2)
                        pe.wait_ge(kr_done, s - 1)
                    b = 2 * (s % 2)
                    for k in range(DK):
                        if s == 0 and k % 2 == 0:
                            pe.wait_ge(w_split, k // 2 + 1)
                        lhs = tuple(u[:, k, s * P:(s + 1) * P] for u in (c.u_hi, c.u_lo))
                        mm3(pe, c.ps[:, b, :], lhs, tuple(w[:, k, 0:HALF] for w in (w_hi, w_lo)), k == 0, k == DK - 1)
                        last = mm3(pe, c.ps[:, b + 1, 0:LAT - HALF], lhs, tuple(w[:, k, HALF:LAT] for w in (w_hi, w_lo)),
                                   k == 0, k == DK - 1)
                    last.then_inc(proj_done, 1)
                t = s - 1
                if 0 <= t < NT:
                    pe.wait_ge(scaled, 2 * t + 2)
                    pe.wait_ge(kr_done, t + 1)
                    if t >= 2:
                        pe.wait_ge(c_split, t - 1)
                    for i in range(QC):
                        pe.transpose(c.ps[:, 4 + 2 * (t % 2), i * P:(i + 1) * P], lat[:, t % 2, i * P:(i + 1) * P], c.ident[:, :])
                    pe.transpose(c.ps[:, 4 + 2 * (t % 2), QC * P:(QC + 1) * P], kr[:, t % 2, :], c.ident[:, :])
                    for i in range(KC):
                        last = pe.transpose(c.ps[:, 5 + 2 * (t % 2), i * P:(i + 1) * P],
                                            lat[:, t % 2, (QC + i) * P:(QC + i + 1) * P], c.ident[:, :])
                    last.then_inc(turned, 1)


def values(c, tag):
    nc = c.nc
    w_hi_done, w_split = c.sem(tag + "w_hi_done"), c.sem(tag + "w_split")
    v_done = c.sem(tag + "v_done")
    with ExitStack() as own:
        def sb(name, dtype=F32):
            return own.enter_context(nc.sbuf_tensor(tag + name, [P, KC, HEADS, VH], dtype))
        raw, w_hi, w_lo = c.raw_v, sb("w_hi", F32R), sb("w_lo", F32R)
        block = own.enter_context(nc.Block())

        def flat(w, k):
            return w[:, k, :, :].rearrange("p h e -> p (h e)")

        def out(t):
            return c.ps[:, t, :].rearrange("p (h e) -> p h e", e=VH)

        @block.scalar
        def _(act):
            act.wait_ge(c.raw_v_in, 16 * KC)
            split_hi(nc, w_hi[:, :, :, :], raw[:, :, :, :]).then_inc(w_hi_done, 1)
            for t in range(0, NT, 2):
                act.wait_ge(v_done, t + 1)
                nc.scalar.activation(c.v[:, t, :, :], out(t), ACT.Copy)

        @block.vector
        def _(dve):
            dve.wait_ge(w_hi_done, 1)
            split_lo(nc, w_lo[:, :, :, :].rearrange("p k h e -> p (k h e)"),
                     raw[:, :, :, :].rearrange("p k h e -> p (k h e)"),
                     w_hi[:, :, :, :].rearrange("p k h e -> p (k h e)")).then_inc(w_split, 1)
            for t in range(1, NT, 2):
                dve.wait_ge(v_done, t + 1)
                nc.vector.tensor_copy(c.v[:, t, :, :], out(t))

        @block.tensor
        def _(pe):
            pe.wait_ge(w_split, 1)
            for t in range(NT):
                for k in range(KC):
                    lhs = tuple(x[:, k, t * P:(t + 1) * P] for x in (c.ckv_hi, c.ckv_lo))
                    last = mm3(pe, c.ps[:, t, :], lhs, (flat(w_hi, k), flat(w_lo, k)), k == 0, k == KC - 1)
                last.then_inc(v_done, 1)


def attention(c, tag, w_uq, w_ukv):
    nc = c.nc
    scale = float(QK) ** -0.5
    rot_half = ROPE // 2
    NB = NT
    names = ("wq_in", "wkv_in", "w_hi_done", "w_split", "q_done", "k_done", "q_rot", "q_sum", "q_hi", "k_hi", "rope_hi",
             "qk_split", "s_done", "max_done", "neg_done", "p_done", "inv_done", "norm_done", "pt_done", "pt_hi",
             "pt_split", "o_done", "o_read", "v_hi", "v_lo", "pad_zero")
    S = {n: c.sem(tag + n) for n in names}
    with ExitStack() as own:
        def sb(name, shape, dtype=F32):
            return own.enter_context(nc.sbuf_tensor(tag + name, shape, dtype))
        raw_q, raw_kv = sb("raw_q", [P, QC, QK]), sb("raw_kv", [P, KC, P])
        wq_hi, wq_lo = sb("wq_hi", [P, QC, P], F32R), sb("wq_lo", [P, QC, P], F32R)
        wkv_hi, wkv_lo = sb("wkv_hi", [P, KC, P], F32R), sb("wkv_lo", [P, KC, P], F32R)
        qt_hi, qt_lo = sb("qt_hi", [P, SEQ], F32R), sb("qt_lo", [P, SEQ], F32R)
        rot, rot2 = sb("rot", [P, SEQ]), sb("rot2", [P, SEQ])
        probs = sb("probs", [P, 2, SEQ])
        pt_hi, pt_lo = sb("pt_hi", [P, NT, 2, P], F32R), sb("pt_lo", [P, NT, 2, P], F32R)
        v_hi, v_lo = sb("v_hi", [P, NT, VH], F32R), sb("v_lo", [P, NT, VH], F32R)
        mx, neg, rs, inv = (sb(n, [P, NB]) for n in ("mx", "neg", "rs", "inv"))
        block = own.enter_context(nc.Block())

        def two(b):
            return c.ps[:, b:b + 2, :].rearrange("p b f -> p (b f)")

        def head(x, h):
            return x[:, :, bass.ds(h, 1), :].rearrange("p k o e -> p k (o e)")

        def later(g, r):
            return not isinstance(g, int) or g > 0 or r > 0

        def heads(eng, body):
            for r in range(2):
                body(0, r, False)
            with eng.Fori(1, HEADS // 2 - 1) as g:
                for r in range(2):
                    body(g, r, False)
            for r in range(2):
                body(HEADS // 2 - 1, r, r == 1)

        def turned(i):
            return two(0)[:, 0:(i + 1) * P].rearrange("p (j q) -> p j q", q=P)

        pieces = ((0, QK, 0), (QK, rot_half, NOPE + rot_half), (QK + rot_half, rot_half, NOPE))

        @block.sync
        def _(sp):
            vq = w_uq.rearrange("(k p) (h e) -> p k h e", p=P, h=HEADS)
            vkv = w_ukv.rearrange("(k p) (h e) -> p k h e", p=P, h=HEADS)

            def load(h):
                sp.dma_start(raw_q[:, :, :], head(vq, h)).then_inc(S["wq_in"], 16)
                sp.dma_start(raw_kv[:, :, :], head(vkv, h)).then_inc(S["wkv_in"], 16)
            load(0)
            with sp.Fori(1, HEADS) as h:
                sp.wait_ge(S["w_split"], h + 0)
                load(h)

        @block.scalar
        def _(act):
            def weights(g, r):
                act.wait_ge(S["wq_in"], g * 32 + (16 * r + 16))
                if later(g, r):
                    act.wait_ge(S["k_done"], g * 4 + 2 * r)
                for to, w, at in pieces:
                    split_hi(nc, wq_hi[:, :, to:to + w], raw_q[:, :, at:at + w])
                act.wait_ge(S["wkv_in"], g * 32 + (16 * r + 16))
                split_hi(nc, wkv_hi[:, :, :], raw_kv[:, :, :]).then_inc(S["w_hi_done"], 1)

            def project(g, r):
                for hf in range(2):
                    cols = slice(hf * HALF, (hf + 1) * HALF)
                    act.wait_ge(S["q_done"], g * 4 + (2 * r + hf + 1))
                    split_hi(nc, qt_hi[0:NOPE, cols], c.ps[0:NOPE, 4 + hf, :]).then_inc(S["q_hi"], 1)
                for hf in range(2):
                    cols = slice(hf * HALF, (hf + 1) * HALF)
                    act.wait_ge(S["q_sum"], g * 4 + (2 * r + hf + 1))
                    split_hi(nc, qt_hi[NOPE:QK, cols], rot[NOPE:QK, cols]).then_inc(S["rope_hi"], 1)
                for hf in range(2):
                    cols = slice(hf * HALF, (hf + 1) * HALF)
                    act.wait_ge(S["k_done"], g * 4 + (2 * r + hf + 1))
                    split_hi(nc, c.kt_hi[0:NOPE, cols], c.ps[0:NOPE, 6 + hf, :]).then_inc(S["k_hi"], 1)

            def take(g, r, m):
                act.wait_ge(S["o_done"], g * 8 + (4 * r + m + 1))
                dst = c.o_t[r * VH:(r + 1) * VH, bass.ds(g, 1), 2 * m * P:(2 * m + 2) * P].rearrange("p o q -> p (o q)")
                nc.scalar.activation(dst, c.ps[0:VH, 2 + m % 2, 0:2 * P], ACT.Copy).then_inc(S["o_read"], 1)

            act.wait_ge(S["pad_zero"], 1)
            for x in (qt_hi, qt_lo, c.kt_hi, c.kt_lo):
                split_hi(nc, x[QK:P, :], rot[QK:P, :])
            weights(0, 0)
            project(0, 0)

            def body(g, r, last):
                for s in range(NB + 1):
                    if s < NB:
                        w = (s + 1) * P
                        act.wait_ge(S["neg_done"], g * 16 + (8 * r + s + 1))
                        if s >= 2 or later(g, r):
                            act.wait_ge(S["pt_done"], g * 16 + (8 * r + s - 1))
                        nc.scalar.activation(probs[:, s % 2, 0:w], two(4 + 2 * (s % 2))[:, 0:w], ACT.Exp, bias=neg[:, s:s + 1],
                                             scale=scale, accum_out=rs[:, s:s + 1]).then_inc(S["p_done"], 1)
                    elif not last:
                        project(g + 1 if r else g, 1 - r)
                    if s == 1 and later(g, r):
                        take(g if r else g - 1, 1 - r, 3)
                    if s in (3, 5, 7):
                        take(g, r, (s - 3) // 2)
                    i = s - 1
                    if i >= 0:
                        act.wait_ge(S["pt_done"], g * 16 + (8 * r + i + 1))
                        if i >= 2 or later(g, r):
                            act.wait_ge(S["o_done"], g * 8 + (4 * r + i // 2))
                        split_hi(nc, pt_hi[:, 0:i + 1, i % 2, :], turned(i)).then_inc(S["pt_hi"], 1)
                    if s == 2:
                        split_hi(nc, v_hi[:, :, :], head(c.v, g * 2 + r)).then_inc(S["v_hi"], 1)
                    if s == 4 and not last:
                        weights(g + 1 if r else g, 1 - r)
            heads(act, body)
            take(HEADS // 2 - 1, 1, 3)

        @block.gpsimd
        def _(pool):
            nc.gpsimd.memset(rot[QK:P, :], 0.0).then_inc(S["pad_zero"], 1)
            with pool.Fori(0, HEADS) as h:
                for hf in range(2):
                    cols = slice(hf * HALF, (hf + 1) * HALF)
                    pool.wait_ge(S["q_rot"], h * 4 + (2 * hf + 2))
                    nc.gpsimd.tensor_tensor(rot[NOPE:QK, cols], rot[NOPE:QK, cols], rot2[NOPE:QK, cols], ALU.add)\
                        .then_inc(S["q_sum"], 1)

        @block.vector
        def _(dve):
            def weights(g, r):
                dve.wait_ge(S["w_hi_done"], g * 2 + (r + 1))
                for to, w, at in pieces:
                    split_lo(nc, wq_lo[:, :, to:to + w], raw_q[:, :, at:at + w], wq_hi[:, :, to:to + w])
                split_lo(nc, wkv_lo[:, :, :], raw_kv[:, :, :], wkv_hi[:, :, :]).then_inc(S["w_split"], 1)

            def project(g, r):
                for hf in range(2):
                    cols = slice(hf * HALF, (hf + 1) * HALF)
                    dve.wait_ge(S["q_done"], g * 4 + (2 * r + hf + 1))
                    nc.vector.tensor_tensor(rot2[NOPE:QK, cols], c.ps[QK:P, 4 + hf, :], c.trig[QK:P, cols], ALU.mult)\
                        .then_inc(S["q_rot"], 1)
                    nc.vector.tensor_tensor(rot[NOPE:QK, cols], c.ps[NOPE:QK, 4 + hf, :], c.trig[NOPE:QK, cols], ALU.mult)\
                        .then_inc(S["q_rot"], 1)
                    dve.wait_ge(S["q_hi"], g * 4 + (2 * r + hf + 1))
                    split_lo(nc, qt_lo[0:NOPE, cols], c.ps[0:NOPE, 4 + hf, :], qt_hi[0:NOPE, cols])
                for hf in range(2):
                    cols = slice(hf * HALF, (hf + 1) * HALF)
                    dve.wait_ge(S["rope_hi"], g * 4 + (2 * r + hf + 1))
                    split_lo(nc, qt_lo[NOPE:QK, cols], rot[NOPE:QK, cols], qt_hi[NOPE:QK, cols])
                for hf in range(2):
                    cols = slice(hf * HALF, (hf + 1) * HALF)
                    dve.wait_ge(S["k_hi"], g * 4 + (2 * r + hf + 1))
                    split_lo(nc, c.kt_lo[0:NOPE, cols], c.ps[0:NOPE, 6 + hf, :], c.kt_hi[0:NOPE, cols]).then_inc(S["qk_split"], 1)

            weights(0, 0)
            project(0, 0)

            def body(g, r, last):
                for s in range(NB + 1):
                    if s < NB:
                        w = (s + 1) * P
                        n = g * 16 + (8 * r + s + 1)
                        dve.wait_ge(S["s_done"], n)
                        nc.vector.tensor_reduce(mx[:, s:s + 1], two(4 + 2 * (s % 2))[:, 0:w], AX_X, ALU.max)\
                            .then_inc(S["max_done"], 1)
                        dve.wait_ge(S["max_done"], n)
                        nc.vector.tensor_scalar(neg[:, s:s + 1], mx[:, s:s + 1], -scale, None, ALU.mult)\
                            .then_inc(S["neg_done"], 1)
                        dve.wait_ge(S["p_done"], n)
                        nc.vector.reciprocal(inv[:, s:s + 1], rs[:, s:s + 1]).then_inc(S["inv_done"], 1)
                        dve.wait_ge(S["inv_done"], n)
                        nc.vector.tensor_scalar(probs[:, s % 2, 0:w], probs[:, s % 2, 0:w], inv[:, s:s + 1], None, ALU.mult)\
                            .then_inc(S["norm_done"], 1)
                    elif not last:
                        project(g + 1 if r else g, 1 - r)
                    i = s - 1
                    if i >= 0:
                        dve.wait_ge(S["pt_hi"], g * 16 + (8 * r + i + 1))
                        split_lo(nc, pt_lo[:, 0:i + 1, i % 2, :], turned(i), pt_hi[:, 0:i + 1, i % 2, :]).then_inc(S["pt_split"], 1)
                    if s == 2:
                        dve.wait_ge(S["v_hi"], g * 2 + (r + 1))
                        split_lo(nc, v_lo[:, :, :], head(c.v, g * 2 + r), v_hi[:, :, :]).then_inc(S["v_lo"], 1)
                    if s == 4 and not last:
                        weights(g + 1 if r else g, 1 - r)
            heads(dve, body)

        @block.tensor
        def _(pe):
            def project(g, r):
                pe.wait_ge(S["w_split"], g * 2 + (r + 1))
                for n, (weights, x, chunks, signal) in enumerate((
                        ((wq_hi, wq_lo), (c.cq_hi, c.cq_lo), QC, S["q_done"]),
                        ((wkv_hi, wkv_lo), (c.ckv_hi, c.ckv_lo), KC, S["k_done"]))):
                    if later(g, r):
                        pe.wait_ge(S["p_done"], g * 16 + (8 * r - 1 + n))
                    for hf in range(2):
                        for k in range(chunks):
                            last = mm3(pe, c.ps[:, 4 + 2 * n + hf, :], tuple(w[:, k, :] for w in weights),
                                       tuple(y[:, k, hf * HALF:(hf + 1) * HALF] for y in x), k == 0, k == chunks - 1)
                        last.then_inc(signal, 1)

            def turn(g, r, i):
                pe.wait_ge(S["norm_done"], g * 16 + (8 * r + i + 1))
                if i > 0 or later(g, r):
                    pe.wait_ge(S["pt_split"], g * 16 + (8 * r + i))
                for j in range(i + 1):
                    last = pe.transpose(c.ps[:, j // 4, (j % 4) * P:(j % 4 + 1) * P], probs[:, i % 2, j * P:(j + 1) * P],
                                        c.ident[:, :])
                last.then_inc(S["pt_done"], 1)

            def product(g, r, m):
                pe.wait_ge(S["pt_split"], g * 16 + (8 * r + 2 * m + 2))
                if m == 0:
                    pe.wait_ge(S["v_lo"], g * 2 + (r + 1))
                if m >= 2 or later(g, r):
                    pe.wait_ge(S["o_read"], g * 8 + (4 * r + m - 1))
                both = [(j, v, pt, slice(0, 2)) for j in range(2 * m + 1)
                        for v, pt in ((v_hi, pt_hi), (v_hi, pt_lo), (v_lo, pt_hi))]
                second = [(2 * m + 1, v, pt, slice(1, 2)) for v, pt in ((v_hi, pt_hi), (v_hi, pt_lo), (v_lo, pt_hi))]
                passes = both[:1] + second + both[1:]
                for n, (j, v, pt, blocks) in enumerate(passes):
                    last = pe.matmul(c.ps[0:VH, 2 + m % 2, blocks.start * P:2 * P], v[:, j, :],
                                     pt[:, j, blocks, :].rearrange("p b q -> p (b q)"), start=n == 0, stop=n == len(passes) - 1)
                last.then_inc(S["o_done"], 1)

            project(0, 0)

            def body(g, r, last):
                for s in range(NB + 1):
                    if s < NB:
                        if s == 0:
                            pe.wait_ge(S["qk_split"], g * 4 + (2 * r + 2))
                        if s >= 2:
                            pe.wait_ge(S["p_done"], g * 16 + (8 * r + s - 1))
                        q = tuple(x[:, s * P:(s + 1) * P] for x in (qt_hi, qt_lo))
                        for at in range(0, (s + 1) * P, HALF):
                            w = min(HALF, (s + 1) * P - at)
                            out = c.ps[:, 4 + 2 * (s % 2) + at // HALF, 0:w]
                            mm3(pe, out, q, tuple(x[:, at:at + w] for x in (c.kt_hi, c.kt_lo)), True, True)
                        at = s * P % HALF
                        pe.matmul(c.ps[:, 4 + 2 * (s % 2) + s // 4, at:at + P], c.ident_r[:, :], c.mask_r[:, :], start=False,
                                  stop=True, skip_group_check=True).then_inc(S["s_done"], 1)
                    elif not last:
                        project(g + 1 if r else g, 1 - r)
                    if s == 1 and later(g, r):
                        product(g if r else g - 1, 1 - r, 3)
                    if s in (3, 5, 7):
                        product(g, r, (s - 3) // 2)
                    if s >= 1:
                        turn(g, r, s - 1)
            heads(pe, body)
            product(HEADS // 2 - 1, 1, 3)


def split_heads(c):
    nc = c.nc
    hi_done = c.sem("heads_hi_done")
    with nc.Block() as block:
        @block.scalar
        def _(act):
            for k in range(HEADS * VH // P):
                split_hi(nc, c.o_hi[:, k, :], c.o_t[:, k, :]).then_inc(hi_done, 1)

        @block.vector
        def _(dve):
            for k in range(HEADS * VH // P):
                dve.wait_ge(hi_done, k + 1)
                split_lo(nc, c.o_lo[:, k, :], c.o_t[:, k, :], c.o_hi[:, k, :])


def gated(c, tag, gate_w, branch_w, x, chunks, store=None, addend=None, merged=None):
    nc = c.nc
    names = ("gate_in", "branch_in", "w_hi_done", "w_split", "gate_done", "branch_done", "sig_done", "prod_done", "stored",
             "add_in", "add_done")
    S = {n: c.sem(tag + n) for n in names}
    with ExitStack() as own:
        def sb(name, shape, dtype=F32):
            return own.enter_context(nc.sbuf_tensor(tag + name, shape, dtype))
        raw_g, raw_b = sb("raw_g", [P, DK, P]), sb("raw_b", [P, chunks, P])
        g_hi, g_lo = sb("g_hi", [P, DK, P], F32R), sb("g_lo", [P, DK, P], F32R)
        b_hi, b_lo = sb("b_hi", [P, chunks, P], F32R), sb("b_lo", [P, chunks, P], F32R)
        sig, prod = sb("sig", [P, 2, HALF]), sb("prod", [P, 2, HALF])
        if addend is not None:
            other = sb("other", [P, 2, HALF])
        block = own.enter_context(nc.Block())
        gate_view = gate_w.rearrange("(k p) f -> p k f", p=P)
        branch_view = branch_w.rearrange("(k p) f -> p k f", p=P)

        def looped(eng, body):
            body(0, False)
            with eng.Fori(1, DK - 1) as d:
                body(d, False)
            body(DK - 1, True)

        def later(d):
            return not isinstance(d, int) or d > 0

        @block.sync
        def _(sp):
            def load(d):
                if later(d):
                    sp.wait_ge(S["w_split"], d * 2)
                sp.dma_start(raw_g[:, :, :], gate_view[:, :, bass.ts(d, P)]).then_inc(S["gate_in"], 16)
                sp.dma_start(raw_b[:, :, :], branch_view[:, :, bass.ts(d, P)]).then_inc(S["branch_in"], 16)
                if addend is not None:
                    if later(d):
                        sp.wait_ge(S["add_done"], d * 2)
                    sp.dma_start(other[:, :, :], addend[bass.ts(d, P), :].rearrange("p (a f) -> p a f", a=2))\
                        .then_inc(S["add_in"], 16)

            def save(d):
                sp.wait_ge(S["prod_done"], d * 2 + 2)
                sp.dma_start(store[bass.ts(d, P), :].rearrange("p (a f) -> p a f", a=2), prod[:, :, :]).then_inc(S["stored"], 16)

            load(0)

            def body(d, last):
                if not last:
                    load(d + 1)
                if store is not None:
                    save(d)
            looped(sp, body)
            if store is not None:
                sp.wait_ge(S["stored"], 16 * DK)

        @block.scalar
        def _(act):
            def hi(d):
                act.wait_ge(S["gate_in"], d * 16 + 16)
                if later(d):
                    act.wait_ge(S["gate_done"], d * 2)
                split_hi(nc, g_hi[:, :, :], raw_g[:, :, :]).then_inc(S["w_hi_done"], 1)
                act.wait_ge(S["branch_in"], d * 16 + 16)
                if later(d):
                    act.wait_ge(S["branch_done"], d * 2)
                split_hi(nc, b_hi[:, :, :], raw_b[:, :, :]).then_inc(S["w_hi_done"], 1)

            hi(0)

            def body(d, last):
                for hf in range(2):
                    act.wait_ge(S["gate_done"], d * 2 + (hf + 1))
                    if later(d):
                        act.wait_ge(S["prod_done"], d * 2 + (hf - 1))
                    nc.scalar.activation(sig[:, hf, :], c.ps[:, hf, :], ACT.Sigmoid).then_inc(S["sig_done"], 1)
                if not last:
                    hi(d + 1)
            looped(act, body)

        @block.vector
        def _(dve):
            def lo(d):
                dve.wait_ge(S["w_hi_done"], d * 2 + 1)
                split_lo(nc, g_lo[:, :, :], raw_g[:, :, :], g_hi[:, :, :]).then_inc(S["w_split"], 1)

            def lo_b(d):
                dve.wait_ge(S["w_hi_done"], d * 2 + 2)
                split_lo(nc, b_lo[:, :, :], raw_b[:, :, :], b_hi[:, :, :]).then_inc(S["w_split"], 1)

            lo(0)
            lo_b(0)

            def body(d, last):
                if not last:
                    lo(d + 1)
                for hf in range(2):
                    dve.wait_ge(S["sig_done"], d * 2 + (hf + 1))
                    dve.wait_ge(S["branch_done"], d * 2 + (hf + 1))
                    if later(d) and store is not None:
                        dve.wait_ge(S["stored"], d * 16)
                    if later(d) and store is None:
                        dve.wait_ge(S["add_done"], d * 2 + (hf - 1))
                    nc.vector.tensor_tensor(prod[:, hf, :], sig[:, hf, :], c.ps[:, 2 + hf, :], ALU.mult)\
                        .then_inc(S["prod_done"], 1)
                if not last:
                    lo_b(d + 1)
            looped(dve, body)

        if addend is not None:
            @block.gpsimd
            def _(pool):
                def body(d, last):
                    pool.wait_ge(S["add_in"], d * 16 + 16)
                    for hf in range(2):
                        pool.wait_ge(S["prod_done"], d * 2 + (hf + 1))
                        dst = merged[:, bass.ds(d, 1), hf * HALF:(hf + 1) * HALF].rearrange("p o f -> p (o f)")
                        nc.gpsimd.tensor_tensor(dst, prod[:, hf, :], other[:, hf, :], ALU.add).then_inc(S["add_done"], 1)
                looped(pool, body)

        @block.tensor
        def _(pe):
            def body(d, last):
                pe.wait_ge(S["w_split"], d * 2 + 1)
                for hf in range(2):
                    if later(d):
                        pe.wait_ge(S["sig_done"], d * 2 + (hf - 1))
                    for k in range(DK):
                        ins = mm3(pe, c.ps[:, hf, :], (g_hi[:, k, :], g_lo[:, k, :]),
                                  tuple(u[:, k, hf * HALF:(hf + 1) * HALF] for u in (c.u_hi, c.u_lo)), k == 0, k == DK - 1)
                    ins.then_inc(S["gate_done"], 1)
                pe.wait_ge(S["w_split"], d * 2 + 2)
                for hf in range(2):
                    if later(d):
                        pe.wait_ge(S["prod_done"], d * 2 + (hf - 1))
                    for k in range(chunks):
                        ins = mm3(pe, c.ps[:, 2 + hf, :], (b_hi[:, k, :], b_lo[:, k, :]),
                                  tuple(y[:, k, hf * HALF:(hf + 1) * HALF] for y in x), k == 0, k == chunks - 1)
                    ins.then_inc(S["branch_done"], 1)
            looped(pe, body)


def recurrence(c, tag, w_xb, w_yb, w_rg, w_ig):
    nc = c.nc
    names = ("x_in", "y_in", "gates_in", "w_hi_done", "w_split", "x_done", "y_done", "r_done", "i_done", "conv", "conv_done",
             "xc_hi", "xc_split", "gelu_done", "sig_r", "sig_i", "a_done", "tanh_done", "m_done", "root_done", "ix_done",
             "bx_done", "scan_done", "out_done", "out_hi", "out_split")
    S = {n: c.sem(tag + n) for n in names}
    with ExitStack() as own:
        def sb(name, shape, dtype=F32):
            return own.enter_context(nc.sbuf_tensor(tag + name, shape, dtype))
        raw = {"x": sb("raw_x", [P, DK, P]), "y": sb("raw_y", [P, DK, P]), "g": sb("raw_g", [P, 2, P])}
        w_hi = {"x": sb("x_hi", [P, DK, P], F32R), "y": sb("y_hi", [P, DK, P], F32R), "g": sb("g_hi", [P, 2, P], F32R)}
        w_lo = {"x": sb("x_lo", [P, DK, P], F32R), "y": sb("y_lo", [P, DK, P], F32R), "g": sb("g_lo", [P, 2, P], F32R)}
        xc, gate_y, r, bx, a, a2, hid = (sb(n, [P, SEQ]) for n in ("xc", "gate_y", "r", "bx", "a", "a2", "hid"))
        xc_hi, xc_lo = sb("xc_hi", [P, SEQ], F32R), sb("xc_lo", [P, SEQ], F32R)
        block = own.enter_context(nc.Block())
        order = ("x", "y", "g")

        def two(b):
            return c.ps[:, b:b + 2, :].rearrange("p b f -> p (b f)")

        def col(row, d):
            return c.params[:, bass.ds(d + row, 1)]

        def later(d):
            return not isinstance(d, int) or d > 0

        def looped(eng, body):
            body(0, 2)
            with eng.Fori(1, DK - 2) as d:
                body(d, 2)
            body(DK - 2, 1)
            body(DK - 1, 0)

        @block.sync
        def _(sp):
            vx, vy = (w.rearrange("(k p) f -> p k f", p=P) for w in (w_xb, w_yb))

            def load(d):
                for n, (key, signal) in enumerate((("x", "x_in"), ("y", "y_in"), ("g", "gates_in"))):
                    if later(d):
                        sp.wait_ge(S["w_split"], d * 3 + (n - 2))
                    if key == "g":
                        for i, w in enumerate((w_rg, w_ig)):
                            sp.dma_start(raw["g"][:, i, :], w[bass.ds(d, 1), :, :].rearrange("o i j -> (o i) j"))\
                                .then_inc(S[signal], 16)
                    else:
                        sp.dma_start(raw[key][:, :, :], (vx if key == "x" else vy)[:, :, bass.ts(d, P)]).then_inc(S[signal], 16)
            load(0)

            def body(d, more):
                if more:
                    load(d + 1)
            looped(sp, body)

        @block.scalar
        def _(act):
            def hi(key, d):
                used = {"x": "x_done", "y": "y_done", "g": "i_done"}[key]
                arrived = {"x": "x_in", "y": "y_in", "g": "gates_in"}[key]
                n = 32 if key == "g" else 16
                act.wait_ge(S[arrived], d * n + n)
                if later(d):
                    act.wait_ge(S[used], d * 2)
                split_hi(nc, w_hi[key][:, :, :], raw[key][:, :, :]).then_inc(S["w_hi_done"], 1)

            def conv_hi(d):
                act.wait_ge(S["conv_done"], d + 1)
                if later(d):
                    act.wait_ge(S["i_done"], d * 2)
                split_hi(nc, xc_hi[:, :], xc[:, :]).then_inc(S["xc_hi"], 1)

            for key in order:
                hi(key, 0)
            conv_hi(0)
            hi("x", 1)

            def body(d, more):
                act.wait_ge(S["y_done"], d * 2 + 2)
                if later(d):
                    act.wait_ge(S["out_split"], d + 0)
                nc.scalar.activation(gate_y[:, :], two(2), ACT.Gelu_apprx_tanh).then_inc(S["gelu_done"], 1)
                if more:
                    hi("y", d + 1)
                act.wait_ge(S["r_done"], d * 2 + 2)
                nc.scalar.activation(r[:, :], two(4), ACT.Sigmoid, bias=col(ROW_B_RG, d)).then_inc(S["sig_r"], 1)
                act.wait_ge(S["i_done"], d * 2 + 2)
                if later(d):
                    act.wait_ge(S["scan_done"], d + 0)
                nc.scalar.activation(bx[:, :], two(6), ACT.Sigmoid, bias=col(ROW_B_IG, d)).then_inc(S["sig_i"], 1)
                if more:
                    hi("g", d + 1)
                act.wait_ge(S["sig_r"], d + 1)
                nc.scalar.activation(a[:, :], r[:, :], ACT.Exp, scale=c.rates[:, 0, bass.ds(d, 1)])
                nc.scalar.activation(a2[:, :], r[:, :], ACT.Exp, scale=c.rates[:, 1, bass.ds(d, 1)]).then_inc(S["a_done"], 1)
                act.wait_ge(S["a_done"], d + 1)
                nc.scalar.activation(r[:, :], r[:, :], ACT.Tanh, scale=c.rates[:, 2, bass.ds(d, 1)]).then_inc(S["tanh_done"], 1)
                act.wait_ge(S["m_done"], d + 1)
                nc.scalar.activation(r[:, :], r[:, :], ACT.Sqrt).then_inc(S["root_done"], 1)
                if more:
                    conv_hi(d + 1)
                if more == 2:
                    hi("x", d + 2)
                act.wait_ge(S["out_done"], d + 1)
                split_hi(nc, c.lru_hi[:, bass.ds(d, 1), :].rearrange("p o f -> p (o f)"), gate_y[:, :]).then_inc(S["out_hi"], 1)
            looped(act, body)

        @block.vector
        def _(dve):
            def lo(n, key, d):
                dve.wait_ge(S["w_hi_done"], d * 3 + (n + 1))
                split_lo(nc, w_lo[key][:, :, :], raw[key][:, :, :], w_hi[key][:, :, :]).then_inc(S["w_split"], 1)

            def convolve(d):
                dve.wait_ge(S["x_done"], d * 2 + 2)
                if later(d):
                    dve.wait_ge(S["ix_done"], d + 0)
                taps = CONV - 1
                nc.vector.tensor_scalar(xc[:, :], two(0), col(ROW_CONV_W + taps * DK, d), col(ROW_CONV_B, d),
                                        ALU.mult, ALU.add).then_inc(S["conv"], 1)
                for k in range(taps):
                    back = taps - k
                    dve.wait_ge(S["conv"], d * taps + (k + 1))
                    nc.vector.scalar_tensor_tensor(
                        out=xc[:, back:SEQ], in0=two(0)[:, 0:SEQ - back], scalar=col(ROW_CONV_W + k * DK, d),
                        in1=xc[:, back:SEQ], op0=ALU.mult, op1=ALU.add).then_inc(S["conv_done" if k == taps - 1 else "conv"], 1)
                dve.wait_ge(S["xc_hi"], d + 1)
                split_lo(nc, xc_lo[:, :], xc[:, :], xc_hi[:, :]).then_inc(S["xc_split"], 1)

            for n, key in enumerate(order):
                lo(n, key, 0)
            convolve(0)
            lo(0, "x", 1)

            def body(d, more):
                if more:
                    lo(1, "y", d + 1)
                    lo(2, "g", d + 1)
                dve.wait_ge(S["tanh_done"], d + 1)
                nc.vector.scalar_tensor_tensor(out=r[:, :], in0=a2[:, :], scalar=1.0, in1=r[:, :], op0=ALU.add,
                                               op1=ALU.mult).then_inc(S["m_done"], 1)
                if more:
                    convolve(d + 1)
                if more == 2:
                    lo(0, "x", d + 2)
                dve.wait_ge(S["bx_done"], d + 1)
                if later(d):
                    dve.wait_ge(S["out_done"], d + 0)
                nc.vector.tensor_tensor_scan(hid[:, :], a[:, :], bx[:, :], 0.0, ALU.mult, ALU.add).then_inc(S["scan_done"], 1)
                dve.wait_ge(S["out_hi"], d + 1)
                one = (slice(None), bass.ds(d, 1), slice(None))
                split_lo(nc, c.lru_lo[one].rearrange("p o f -> p (o f)"), gate_y[:, :],
                         c.lru_hi[one].rearrange("p o f -> p (o f)")).then_inc(S["out_split"], 1)
            looped(dve, body)

        @block.gpsimd
        def _(pool):
            def body(d, more):
                pool.wait_ge(S["sig_i"], d + 1)
                nc.gpsimd.tensor_tensor(bx[:, :], bx[:, :], xc[:, :], ALU.mult).then_inc(S["ix_done"], 1)
                pool.wait_ge(S["root_done"], d + 1)
                pool.wait_ge(S["ix_done"], d + 1)
                nc.gpsimd.tensor_tensor(bx[:, :], bx[:, :], r[:, :], ALU.mult).then_inc(S["bx_done"], 1)
                pool.wait_ge(S["scan_done"], d + 1)
                pool.wait_ge(S["gelu_done"], d + 1)
                nc.gpsimd.tensor_tensor(gate_y[:, :], hid[:, :], gate_y[:, :], ALU.mult).then_inc(S["out_done"], 1)
            looped(pool, body)

        @block.tensor
        def _(pe):
            def body(d, more):
                for n, (key, signal, free) in enumerate((("x", "x_done", "conv_done"), ("y", "y_done", "gelu_done"))):
                    pe.wait_ge(S["w_split"], d * 3 + (n + 1))
                    if later(d):
                        pe.wait_ge(S[free], d + 0)
                    for hf in range(2):
                        for k in range(DK):
                            ins = mm3(pe, c.ps[:, 2 * n + hf, :], (w_hi[key][:, k, :], w_lo[key][:, k, :]),
                                      tuple(u[:, k, hf * HALF:(hf + 1) * HALF] for u in (c.u_hi, c.u_lo)), k == 0, k == DK - 1)
                        ins.then_inc(S[signal], 1)
                pe.wait_ge(S["w_split"], d * 3 + 3)
                pe.wait_ge(S["xc_split"], d + 1)
                for i, (signal, free) in enumerate((("r_done", "sig_r"), ("i_done", "sig_i"))):
                    if later(d):
                        pe.wait_ge(S[free], d + 0)
                    for hf in range(2):
                        cols = slice(hf * HALF, (hf + 1) * HALF)
                        mm3(pe, c.ps[:, 4 + 2 * i + hf, :], (w_hi["g"][:, i, :], w_lo["g"][:, i, :]),
                            (xc_hi[:, cols], xc_lo[:, cols]), True, True).then_inc(S[signal], 1)
            looped(pe, body)


def out_projection(c, tag, w_out, merged):
    nc = c.nc
    raw_in = [c.sem(f"{tag}raw_in{i}") for i in range(2)]
    names = ("m_hi", "m_split", "w_hi_done", "w_split", "w_used", "y_act", "y_dve")
    S = {n: c.sem(tag + n) for n in names}
    with ExitStack() as own:
        def sb(name, shape, dtype=F32):
            return own.enter_context(nc.sbuf_tensor(tag + name, shape, dtype))
        raw = sb("raw", [P, 2, D])
        w_hi, w_lo = c.w_hi, c.w_lo
        block = own.enter_context(nc.Block())
        steps = [(th, k) for th in range(2) for k in range(DK)]

        def evacuate(eng, th):
            eng.wait_ge(S["w_used"], DK * (th + 1))
            for tt in range(4):
                if eng is nc.scalar:
                    nc.scalar.activation(c.y[:, 4 * th + tt, 0:HALF], c.ps[:, 2 * tt, :], ACT.Copy).then_inc(S["y_act"], 1)
                else:
                    nc.vector.tensor_copy(c.y[:, 4 * th + tt, HALF:D], c.ps[:, 2 * tt + 1, :]).then_inc(S["y_dve"], 1)

        @block.sync
        def _(sp):
            view = w_out.rearrange("(k p) f -> p k f", p=P)
            for n, (_, k) in enumerate(steps):
                if n >= 2:
                    sp.wait_ge(S["w_split"], n - 1)
                sp.dma_start(raw[:, n % 2, :], view[:, k, :]).then_inc(raw_in[n % 2], 16)

        @block.scalar
        def _(act):
            for n, (th, k) in enumerate(steps):
                if th == 0:
                    split_hi(nc, c.u_hi[:, k, :], merged[:, k, :]).then_inc(S["m_hi"], 1)
                act.wait_ge(raw_in[n % 2], 16 * (n // 2 + 1))
                if n >= 2:
                    act.wait_ge(S["w_used"], n - 1)
                split_hi(nc, w_hi[:, n % 2, :], raw[:, n % 2, :]).then_inc(S["w_hi_done"], 1)
                if k == 0 and th == 1:
                    evacuate(act, 0)
            evacuate(act, 1)

        @block.vector
        def _(dve):
            for n, (th, k) in enumerate(steps):
                if th == 0:
                    dve.wait_ge(S["m_hi"], k + 1)
                    split_lo(nc, c.u_lo[:, k, :], merged[:, k, :], c.u_hi[:, k, :]).then_inc(S["m_split"], 1)
                dve.wait_ge(S["w_hi_done"], n + 1)
                split_lo(nc, w_lo[:, n % 2, :], raw[:, n % 2, :], w_hi[:, n % 2, :]).then_inc(S["w_split"], 1)
                if th == 1 and k == 0:
                    evacuate(dve, 0)
            evacuate(dve, 1)

        @block.tensor
        def _(pe):
            for n, (th, k) in enumerate(steps):
                if th == 0:
                    pe.wait_ge(S["m_split"], k + 1)
                pe.wait_ge(S["w_split"], n + 1)
                for tt in range(4):
                    t = 4 * th + tt
                    for dh in range(2):
                        if th == 1 and k == 0:
                            pe.wait_ge(S["y_dve" if dh else "y_act"], tt + 1)
                        ins = mm3(pe, c.ps[:, 2 * tt + dh, :], tuple(u[:, k, t * P:(t + 1) * P] for u in (c.u_hi, c.u_lo)),
                                  tuple(w[:, n % 2, dh * HALF:(dh + 1) * HALF] for w in (w_hi, w_lo)), k == 0, k == DK - 1)
                ins.then_inc(S["w_used"], 1)


def hybrid_layer(nc, a, out):
    h1 = nc.dram_tensor("h1_scratch", [SEQ, D], F32, kind="Internal").ap()
    mixed = nc.dram_tensor("mixed_scratch", [D, SEQ], F32, kind="Internal").ap()
    with ExitStack() as ctx:
        c = Core(nc, ctx)
        c.ident = c.keep("ident", [P, P])
        c.params, c.rates = c.keep("params", [P, PARAM_ROWS]), c.keep("rates", [P, 3, DK])
        c.ps = ctx.enter_context(nc.psum_tensor("ps", [P, 8, HALF], F32))
        c.u_hi, c.u_lo = c.keep("u_hi", [P, DK, SEQ], F32R), c.keep("u_lo", [P, DK, SEQ], F32R)

        constants(c, a)
        with ExitStack() as own:
            c.res = own.enter_context(nc.sbuf_tensor("f1_res", [P, NT, D], F32))
            ffn_buffers(c, own, "f1_")
            norm_stage(c, "in_", x_dram=a["x"][0], pre_gain=a["ffn1_pre_g"][0],
                       ahead=ffn_ahead(c, "f1_", a["ffn1_w_gate"][0], a["ffn1_w_up"][0]))
            with ExitStack() as streams:
                ffn_streams(c, streams, "f1_")
                ffn_hidden(c, "f1_", a["ffn1_w_gate"][0], a["ffn1_w_up"][0], a["ffn1_w_down"][0])
            norm_stage(c, "mid1_", down=True, post_gain=a["ffn1_post_g"][0], res_gain=0.5,
                       pre_gain=a["mix_pre_g"][0], store=h1)

        c.recycle()
        w_in = a["w_in"][0]
        at_x = LAT
        at_y, at_ga, at_gb = at_x + D, at_x + 2 * D, at_x + 3 * D
        with ExitStack() as own:
            def sb(name, shape, dtype=F32):
                return own.enter_context(nc.sbuf_tensor(name, shape, dtype))
            with ExitStack() as att:
                def sb2(name, shape, dtype=F32):
                    return att.enter_context(nc.sbuf_tensor(name, shape, dtype))
                c.trig = sb2("trig", [P, SEQ])
                c.mask_r, c.ident_r = sb2("mask_r", [P, P], F32R), sb2("ident_r", [P, P], F32R)
                c.cq_hi, c.cq_lo = sb2("cq_hi", [P, QC, SEQ], F32R), sb2("cq_lo", [P, QC, SEQ], F32R)
                c.ckv_hi, c.ckv_lo = sb2("ckv_hi", [P, KC, SEQ], F32R), sb2("ckv_lo", [P, KC, SEQ], F32R)
                c.kt_hi, c.kt_lo = sb2("kt_hi", [P, SEQ], F32R), sb2("kt_lo", [P, SEQ], F32R)
                rope_tables(c, a["positions"][0])
                c.raw_v, c.raw_v_in = sb2("raw_v", [P, KC, HEADS, VH]), c.sem("raw_v_in")
                latents(c, "lat_", w_in, a["w_ukv"][0])
                c.v = sb2("v", [P, NT, HEADS, VH])
                values(c, "val_")
                c.o_t = own.enter_context(nc.sbuf_tensor("o_t", [P, HEADS * VH // P, SEQ], F32, side="right"))
                attention(c, "att_", a["w_uq"][0], a["w_ukv"][0])
            c.o_hi, c.o_lo = (sb(n, [P, HEADS * VH // P, SEQ], F32R) for n in ("o_hi", "o_lo"))
            split_heads(c)
            gated(c, "ga_", w_in[:, at_ga:at_ga + D], a["w_o_mla"][0], (c.o_hi, c.o_lo), HEADS * VH // P, store=mixed)

        c.recycle()
        ffn = ExitStack()
        with ExitStack() as own:
            with ExitStack() as lru:
                c.lru_hi, c.lru_lo = (lru.enter_context(nc.sbuf_tensor(n, [P, DK, SEQ], F32R)) for n in ("lru_hi", "lru_lo"))
                recurrence(c, "lru_", w_in[:, at_x:at_x + D], w_in[:, at_y:at_y + D], a["w_rg"][0], a["w_ig"][0])
                merged = own.enter_context(nc.sbuf_tensor("merged", [P, DK, SEQ], F32, side="right"))
                gated(c, "gb_", w_in[:, at_gb:at_gb + D], a["w_o_lru"][0], (c.lru_hi, c.lru_lo), DK, addend=mixed,
                      merged=merged)
            ffn_buffers(c, ffn, "f2_")
            out_projection(c, "out_", a["w_out"][0], merged)
        c.recycle()
        with ffn:
            c.res = ffn.enter_context(nc.sbuf_tensor("f3_res", [P, NT, D], F32))
            norm_stage(c, "mid2_", x_dram=h1, post_gain=a["mix_post_g"][0], pre_gain=a["ffn2_pre_g"][0],
                       ahead=ffn_ahead(c, "f2_", a["ffn2_w_gate"][0], a["ffn2_w_up"][0]))
            with ExitStack() as streams:
                ffn_streams(c, streams, "f2s_")
                ffn_hidden(c, "f2_", a["ffn2_w_gate"][0], a["ffn2_w_up"][0], a["ffn2_w_down"][0])
            norm_stage(c, "end_", down=True, post_gain=a["ffn2_post_g"][0], res_gain=0.5, store=out[0])


_OUTS = [((1, SEQ, D), "float32")]


def kernel(**inputs):
    import numpy as _np
    import concourse.bacc as _bacc
    from concourse import mybir as _mybir
    from concourse.bass_utils import run_bass_kernel_spmd as _run

    nc = _bacc.Bacc("TRN2", target_bir_lowering=False, num_devices=1)
    arrays, aps = {}, {}
    for name in inputs:
        a = _np.ascontiguousarray(inputs[name])
        arrays[f"in_{name}_dram"] = a
        aps[name] = nc.dram_tensor(f"in_{name}_dram", a.shape, _mybir.dt.from_np(a.dtype), kind="ExternalInput").ap()
    outs = [nc.dram_tensor(f"out_{i}_dram", shape, _mybir.dt.from_np(_np.dtype(dtype)), kind="ExternalOutput").ap()
            for i, (shape, dtype) in enumerate(_OUTS)]
    hybrid_layer(nc, aps, *outs)
    r = _run(nc, [arrays], core_ids=[0])
    got = tuple(r.results[0][f"out_{i}_dram"] for i in range(len(_OUTS)))
    return got[0]
```
